# Optimizing a Trainium2 kernel written in Bass

```python
import jax, jax.numpy as jnp
from jax import lax
import numpy as np

D_MODEL = 2048
BATCH = 1
SEQ = 1024
DEPTH = 1
DEC_BATCH = 8
DEC_SEQ = 1
PAST_LEN = 2048
PAGE_SIZE = 128

HEAD_DIM = 64
D_MIX = D_MODEL
A_HEADS = D_MIX // 2 // HEAD_DIM
B_HEADS = D_MIX // 2 // HEAD_DIM
B_KV_HEADS = B_HEADS // 4
A_WIDTH = A_HEADS * HEAD_DIM
B_WIDTH = B_HEADS * HEAD_DIM
B_KV_WIDTH = B_KV_HEADS * HEAD_DIM
DILATIONS = ((128, 1), (512, 4), (2048, 16))
A_REACH = max(w for w, _ in DILATIONS)
B_WINDOW = 128
BLK = 128
D_PLE = 256
EPS = 1e-6
IN_SPLITS = (A_WIDTH, A_WIDTH, A_WIDTH, A_WIDTH, B_WIDTH, B_KV_WIDTH, B_KV_WIDTH, B_WIDTH)
D_IN = sum(IN_SPLITS)

kernel_name = 'hymba_dilated_swa_sink_decoder_step'

def rms_norm(x, g):
    x32 = x.astype(jnp.float32)
    y = x32 * lax.rsqrt(jnp.mean(x32 * x32, axis=-1, keepdims=True) + EPS) * g.astype(jnp.float32)
    return y.astype(x.dtype)

def alibi_slopes(n):
    return jnp.exp2(-8.0 * jnp.arange(1, n + 1, dtype=jnp.float32) / n)

def softmax_lse(logits, sink):
    m = jnp.max(logits, axis=-1, keepdims=True)
    if sink is not None:
        m = jnp.maximum(m, sink)
    e = jnp.exp(logits - m)
    den = jnp.sum(e, axis=-1, keepdims=True)
    if sink is not None:
        den = den + jnp.exp(sink - m)
    return e / den, (m + jnp.log(den))[..., 0]

def banded_attention(q, k, v, step, n_keys, slopes, sinks):
    assert n_keys <= BLK
    N, L, H, hd = q.shape
    G = k.shape[2]
    R = H // G
    nb = -(-L // BLK)
    Lp = nb * BLK
    pad = lambda a: jnp.pad(a.astype(jnp.float32), ((0, 0), (0, Lp - L), (0, 0), (0, 0)))
    qb = pad(q).reshape(N, nb, BLK, G, R, hd) * (HEAD_DIM ** -0.5)
    kc = pad(k).reshape(N, nb, BLK, G, hd)
    vc = pad(v).reshape(N, nb, BLK, G, hd)
    with_prev = lambda c: jnp.concatenate(
        [jnp.concatenate([jnp.zeros_like(c[:, :1]), c[:, :-1]], axis=1), c], axis=2)
    kk, vv = with_prev(kc), with_prev(vc)
    s = jnp.einsum('nbqgrd,nbkgd->nbgrqk', qb, kk)
    blk = jnp.arange(nb)[:, None, None] * BLK
    qpos = blk + jnp.arange(BLK)[None, :, None]
    kpos = blk - BLK + jnp.arange(2 * BLK)[None, None, :]
    dist = qpos - kpos
    valid = (dist >= 0) & (dist <= n_keys) & (kpos >= 0)
    bias = -slopes.reshape(G, R)[None, :, :, None, None] * (dist * step).astype(jnp.float32)[:, None, None]
    logits = jnp.where(valid[:, None, None], s + bias, -jnp.inf)
    sink = None if sinks is None else sinks.astype(jnp.float32).reshape(G, R, 1, 1)
    p, lse = softmax_lse(logits, sink)
    o = jnp.einsum('nbgrqk,nbkgd->nbqgrd', p, vv).reshape(N, Lp, H, hd)[:, :L]
    lse = lse.transpose(0, 1, 4, 2, 3).reshape(N, Lp, H)[:, :L]
    return o, lse

def dilated_prompt(q, k, v, step, n_keys, slopes):
    B, S, H, hd = q.shape
    Sp = -(-S // step) * step
    def to_sub(a):
        a = jnp.pad(a, ((0, 0), (0, Sp - S), (0, 0), (0, 0)))
        return a.reshape(B, Sp // step, step, *a.shape[2:]).transpose(0, 2, 1, 3, 4).reshape(B * step, Sp // step, *a.shape[2:])
    o, lse = banded_attention(to_sub(q), to_sub(k), to_sub(v), step, n_keys, slopes, None)
    o = o.reshape(B, step, Sp // step, H, hd).transpose(0, 2, 1, 3, 4).reshape(B, Sp, H, hd)[:, :S]
    lse = lse.reshape(B, step, Sp // step, H).transpose(0, 2, 1, 3).reshape(B, Sp, H)[:, :S]
    return o, lse

def gathered_attention(q, k_ctx, v_ctx, n_past, step, n_keys, slopes, sinks):
    N, T, H, hd = q.shape
    G = k_ctx.shape[2]
    R = H // G
    m = jnp.arange(n_keys + 1)
    idx = n_past + jnp.arange(T)[:, None] - m[None, :] * step
    valid = idx >= 0
    idx = jnp.maximum(idx, 0)
    kg = jnp.take(k_ctx, idx, axis=1).astype(jnp.float32)
    vg = jnp.take(v_ctx, idx, axis=1).astype(jnp.float32)
    qg = q.astype(jnp.float32).reshape(N, T, G, R, hd) * (HEAD_DIM ** -0.5)
    s = jnp.einsum('ntgrd,ntmgd->ntgrm', qg, kg)
    bias = -slopes.reshape(G, R, 1) * (m * step).astype(jnp.float32)
    logits = jnp.where(valid[None, :, None, None, :], s + bias, -jnp.inf)
    sink = None if sinks is None else sinks.astype(jnp.float32).reshape(G, R, 1)
    p, lse = softmax_lse(logits, sink)
    o = jnp.einsum('ntgrm,ntmgd->ntgrd', p, vg).reshape(N, T, H, hd)
    return o, lse.reshape(N, T, H)

def combine_patterns(results):
    outs = jnp.stack([o for o, _ in results])
    w = jax.nn.softmax(jnp.stack([l for _, l in results]), axis=0)
    return jnp.sum(w[..., None] * outs, axis=0)

def mixer_inputs(x, g_mix, w_in):
    z = rms_norm(x, g_mix) @ w_in
    qa, ka, va, ga, qb, kb, vb, gb = jnp.split(z, list(np.cumsum(IN_SPLITS)[:-1]), axis=-1)
    heads = lambda t: t.reshape(*t.shape[:-1], t.shape[-1] // HEAD_DIM, HEAD_DIM)
    return heads(qa), heads(ka), heads(va), ga, heads(qb), heads(kb), heads(vb), gb

def mixer_output(x, oa, ob, ga, gb, p, w_out, g_ple, w_pg, w_ple):
    ya = oa.reshape(*oa.shape[:-2], A_WIDTH).astype(x.dtype) * jax.nn.silu(ga)
    yb = ob.reshape(*ob.shape[:-2], B_WIDTH).astype(x.dtype) * jax.nn.silu(gb)
    h = x + jnp.concatenate([ya, yb], axis=-1) @ w_out
    gate = jax.nn.sigmoid(rms_norm(h, g_ple) @ w_pg)
    return h + (p @ w_ple) * gate

def setup_inputs(seed: int = 0) -> dict:
    key = jax.random.key(seed)
    ks = jax.random.split(key, 16)
    f32 = jnp.float32
    a_buf = min(A_REACH, PAST_LEN)
    b_buf = min(B_WINDOW, PAST_LEN)
    nrm = lambda k, shape: jax.random.normal(k, shape, f32)
    return {
        'x_prompt': nrm(ks[0], (BATCH, SEQ, D_MODEL)),
        'x_sample': nrm(ks[1], (DEC_BATCH, DEC_SEQ, D_MODEL)),
        'cache_a_k': nrm(ks[2], (DEPTH, DEC_BATCH, a_buf, A_HEADS, HEAD_DIM)),
        'cache_a_v': nrm(ks[3], (DEPTH, DEC_BATCH, a_buf, A_HEADS, HEAD_DIM)),
        'cache_b_k': nrm(ks[4], (DEPTH, DEC_BATCH, b_buf, B_KV_HEADS, HEAD_DIM)),
        'cache_b_v': nrm(ks[5], (DEPTH, DEC_BATCH, b_buf, B_KV_HEADS, HEAD_DIM)),
        'p_prompt': nrm(ks[6], (DEPTH, BATCH, SEQ, D_PLE)),
        'p_sample': nrm(ks[7], (DEPTH, DEC_BATCH, DEC_SEQ, D_PLE)),
        'g_mix': 1.0 + 0.1 * nrm(ks[8], (DEPTH, D_MODEL)),
        'w_in': nrm(ks[9], (DEPTH, D_MODEL, D_IN)) * D_MODEL ** -0.5,
        'sinks': 0.5 * nrm(ks[10], (DEPTH, B_HEADS)),
        'w_out': nrm(ks[11], (DEPTH, A_WIDTH + B_WIDTH, D_MODEL)) * (A_WIDTH + B_WIDTH) ** -0.5,
        'g_ple': 1.0 + 0.1 * nrm(ks[12], (DEPTH, D_MODEL)),
        'w_pg': nrm(ks[13], (DEPTH, D_MODEL, D_MODEL)) * D_MODEL ** -0.5,
        'w_ple': nrm(ks[14], (DEPTH, D_PLE, D_MODEL)) * D_PLE ** -0.5,
        'g_final': 1.0 + 0.1 * nrm(ks[15], (D_MODEL,)),
    }

def reference(x_prompt, x_sample, cache_a_k, cache_a_v, cache_b_k, cache_b_v, p_prompt, p_sample,
              g_mix, w_in, sinks, w_out, g_ple, w_pg, w_ple, g_final):
    slopes_a = alibi_slopes(A_HEADS)
    slopes_b = alibi_slopes(B_HEADS)
    n_past_a = cache_a_k.shape[2]
    n_past_b = cache_b_k.shape[2]
    xp, xs = x_prompt, x_sample
    ak_p, av_p, bk_p, bv_p, ak_s, av_s, bk_s, bv_s = [], [], [], [], [], [], [], []
    for i in range(DEPTH):
        qa, ka, va, ga, qb, kb, vb, gb = mixer_inputs(xp, g_mix[i], w_in[i])
        oa = combine_patterns([dilated_prompt(qa, ka, va, d, w // d, slopes_a) for w, d in DILATIONS])
        ob, _ = banded_attention(qb, kb, vb, 1, B_WINDOW, slopes_b, sinks[i])
        ak_p.append(ka[:, -A_REACH:]); av_p.append(va[:, -A_REACH:])
        bk_p.append(kb[:, -B_WINDOW:]); bv_p.append(vb[:, -B_WINDOW:])
        xp = mixer_output(xp, oa, ob, ga, gb, p_prompt[i], w_out[i], g_ple[i], w_pg[i], w_ple[i])

        qa, ka, va, ga, qb, kb, vb, gb = mixer_inputs(xs, g_mix[i], w_in[i])
        ka_ctx = jnp.concatenate([cache_a_k[i].astype(ka.dtype), ka], axis=1)
        va_ctx = jnp.concatenate([cache_a_v[i].astype(va.dtype), va], axis=1)
        kb_ctx = jnp.concatenate([cache_b_k[i].astype(kb.dtype), kb], axis=1)
        vb_ctx = jnp.concatenate([cache_b_v[i].astype(vb.dtype), vb], axis=1)
        oa = combine_patterns([gathered_attention(qa, ka_ctx, va_ctx, n_past_a, d, w // d, slopes_a, None)
                               for w, d in DILATIONS])
        ob, _ = gathered_attention(qb, kb_ctx, vb_ctx, n_past_b, 1, B_WINDOW, slopes_b, sinks[i])
        ak_s.append(ka); av_s.append(va); bk_s.append(kb); bv_s.append(vb)
        xs = mixer_output(xs, oa, ob, ga, gb, p_sample[i], w_out[i], g_ple[i], w_pg[i], w_ple[i])
    y_prompt = rms_norm(xp, g_final)
    y_sample = rms_norm(xs, g_final)
    return (y_prompt, y_sample,
            jnp.stack(ak_p), jnp.stack(av_p), jnp.stack(bk_p), jnp.stack(bv_p),
            jnp.stack(ak_s), jnp.stack(av_s), jnp.stack(bk_s), jnp.stack(bv_s))


_drawn_inputs = setup_inputs


def setup_inputs(seed=0):
    import zlib

    import numpy as np

    out = dict(_drawn_inputs(seed))
    spreads = {}
    factors = {'sinks': 6.54, 'g_ple': 3.19}
    for name, (base, spread) in spreads.items():
        noise = np.random.default_rng([zlib.crc32(name.encode()), seed]).standard_normal(out[name].shape)
        drawn = base * np.exp(spread * noise) if base else spread * noise
        out[name] = __import__('jax').numpy.asarray(drawn.astype(out[name].dtype))
    for name, factor in factors.items():
        out[name] = (out[name] * factor).astype(out[name].dtype)
    return out
```

```python
from contextlib import ExitStack

import numpy as np
import concourse.bass as bass
from concourse import mybir

F32 = mybir.dt.float32
F32R = mybir.dt.float32r
ALU = mybir.AluOpType
ACT = mybir.ActivationFunctionType
AX = mybir.AxisListType

P = 128
D = 2048
S = 1024
NB = 8
R = S + NB
KT = D // P
T3 = R // 3
HEADS, HD, KVH = 16, 64, 4
NZ = 52
ZQA, ZKA, ZVA, ZGA, ZQB, ZKB, ZVB, ZGB = 0, 8, 16, 24, 32, 40, 42, 44
PLE = 256
EPS = 1e-6
NEG = -1e30
BLK = P
QB = S // BLK
SCALE = HD ** -0.5
ROW_TILES = [(i * P, P) for i in range(S // P)] + [(S, NB)]
PIECES = [[(0, 128), (128, 128), (256, 88)]] * 3

CHUNKS_A = [(b, k0, min(512, (b + 1) * BLK - k0)) for b in range(QB) for k0 in range(0, (b + 1) * BLK, 512)]
CHUNKS_B = [(b, max(b - 1, 0) * BLK, BLK * min(b + 1, 2)) for b in range(QB)]
PAIRS = HEADS // 2
LAG = 2


SPIECES = [(0, 128), (128, 97), (225, 96), (321, 128), (449, 1)]
S_TILES = list(range(ZQA, ZGA)) + list(range(ZQB, ZGB))


def off(kind, b):
    return 0 if kind == "A" else max(b - 1, 0) * BLK


def turn_step(chunks):
    out = []
    for c, (b, _, _) in enumerate(chunks):
        same = [i for i, x in enumerate(chunks) if x[0] == b]
        out.append(same[-1] + LAG + (c - same[0]))
    return out


def last_chunk(chunks, b):
    return max(i for i, x in enumerate(chunks) if x[0] == b)


SETS = [(1920, 1, 128), (1536, 4, 96), (0, 16, 96)]
NEAR, MID, FAR = range(3)
SROWS = [128, 97, 96]
SCOL = [0, 128, 225]
NKA, NKB = 321, 129


def shape_tables():
    p = np.arange(P)[:, None]
    u = np.arange(S)[None, :]
    dist = p + (S - BLK) - u
    c = (dist <= 128).astype(int) + ((dist % 4 == 0) & (dist <= 512)) + (dist % 16 == 0)
    logc = np.where((dist >= 0) & (c > 0), np.log(np.maximum(c, 1)), NEG)
    band = np.where((dist >= 0) & (dist <= 128), 0.0, NEG)[:, S - 2 * BLK:]
    slopes = np.exp2(-8.0 * np.arange(1, HEADS + 1) / HEADS).astype(np.float32)
    f = np.float32
    da = np.concatenate([128 - np.arange(128), 512 - 4 * np.arange(96), [0], 2048 - 16 * np.arange(96)])
    ca = (da <= 128).astype(int) + ((da % 4 == 0) & (da <= 512)) + (da % 16 == 0)
    db = np.concatenate([128 - np.arange(128), [0]])
    sa = (-slopes[:, None] * da.astype(f)[None, :]) + np.log(ca).astype(f)[None, :]
    sb = -slopes[:, None] * db.astype(f)[None, :]
    return {
        "c_ident": np.eye(P, dtype=f),
        "c_negd": (-dist).astype(f),
        "c_logc": (logc * 8).astype(f),
        "c_band": (band * 8).astype(f),
        "c_slope": np.broadcast_to(8 * slopes, (P, HEADS)).astype(f).copy(),
        "c_sbias": np.concatenate([8 * sa, 8 * sb], axis=1).astype(f),
    }


def bcast_rows(row, n):
    return bass.AP(tensor=row.tensor, offset=row.offset, ap=[[0, n]] + [list(x) for x in row.ap[1:]])


def build(nc, a, o):
    (y_prompt, y_sample, ak_p, av_p, bk_p, bv_p, ak_s, av_s, bk_s, bv_s) = o
    w_in = a["w_in"][0].rearrange("(k p) n -> p k n", p=P)
    w_out = a["w_out"][0].rearrange("(k p) n -> p k n", p=P)
    w_pg = a["w_pg"][0].rearrange("(k p) n -> p k n", p=P)
    w_ple = a["w_ple"][0].rearrange("(k p) n -> p k n", p=P)
    x_p, x_s = a["x_prompt"][0], a["x_sample"].rearrange("b t d -> (b t) d")
    p_p, p_s = a["p_prompt"][0, 0], a["p_sample"][0].rearrange("b t d -> (b t) d")
    yp, ys = y_prompt[0], y_sample.rearrange("b t d -> (b t) d")

    z_dram = nc.dram_tensor("z_scratch", [NZ, P, R], F32, kind="Internal").ap()
    h_dram = nc.dram_tensor("h_scratch", [KT, P, R], F32, kind="Internal").ap()
    y_dram = nc.dram_tensor("y_scratch", [R, D], F32, kind="Internal").ap()
    q_dram = nc.dram_tensor("q_scratch", [NB, D], F32, kind="Internal").ap()

    ctx = ExitStack()
    sem_list = {}

    def sem(name):
        if name not in sem_list:
            sem_list[name] = ctx.enter_context(nc.semaphore(name))
        return sem_list[name]

    with ctx:
        def keep(name, shape, dt=F32):
            return ctx.enter_context(nc.sbuf_tensor(name, shape, dt))

        act_hi = keep("act_hi", [P, KT, R], F32R)
        act_lo = keep("act_lo", [P, KT, R], F32R)
        ident = keep("ident", [P, P])
        small = keep("small", [P, 64])
        hi32 = act_hi[:].bitcast(F32)

        psum = ctx.enter_context(nc.psum_tensor("psum", [P, 8, 512], F32))

        def phase(tensors):
            with ExitStack() as st:
                return [st.enter_context(nc.sbuf_tensor(n, s, d)) for n, s, d in tensors]

        x_in, x_n, g_row = phase([("x_in", [P, 2, D], F32), ("x_n", [P, 2, D], F32), ("g_row", [P, D], F32)])
        with ExitStack() as own:
            acc = own.enter_context(nc.sbuf_tensor("acc", [P, R], F32))
            stage, sq, x_cols, ones, w_lo, w_hi, w_raw = phase([
                ("stage", [P, 2, R], F32), ("sq", [P, R], F32), ("x_cols", [P, 2, 9, P], F32), ("ones", [P, P], F32),
                ("w_lo", [P, 2, KT, P], F32R), ("w_hi", [P, 2, KT, P], F32R), ("w_raw", [P, 2, KT, P], F32)])
            u_raw, u_hi, u_lo, pt_hi, pt_lo, h_in, t_gate, t_y, y_nat, gcol = phase([
                ("u_raw", [P, KT + 2, P], F32), ("u_hi", [P, 2, KT + 2, P], F32R), ("u_lo", [P, 2, KT + 2, P], F32R),
                ("pt_hi", [P, 2, R], F32R), ("pt_lo", [P, 2, R], F32R),
                ("h_in", [P, 2, T3], F32), ("t_gate", [P, 2, T3], F32), ("t_y", [P, 2, T3], F32),
                ("y_nat", [P, 2, 3, P], F32), ("gcol", [P, KT], F32)])
            h_stage, = phase([("h_stage", [P, 2, R], F32)])
        zq, zk, zg, zv, v_nat, k_nat, prob, prob_t, bias, negd, mask, slope, sink, mx, yt = phase([
            ("zq", [P, 2, S], F32), ("zk", [P, 2, S], F32), ("zg", [P, 2, S], F32), ("zv", [P, S], F32),
            ("v_nat", [P, 2, QB, P], F32), ("k_nat", [P, 4, P], F32),
            ("prob", [P, 2 * 1024 + 2 * 896], F32), ("prob_t", [P, 2, 512], F32), ("bias", [P, 2, S], F32),
            ("negd", [P, S], F32), ("mask", [P, S], F32), ("slope", [P, HEADS], F32),
            ("sink", [P, HEADS], F32), ("mx", [P, 2, 24], F32), ("yt", [P, 512], F32)])
        zst, zn, sk, sv, skb, svb, q_all, sprod, sprob, sprob_t, sbias, ssink, sc, srow, ysm, ystmp = phase([
            ("zst", [P, NZ, NB], F32), ("zn", [NB, 36, P], F32), ("sk", [P, 3, S], F32),
            ("sv", [P, 3, S], F32), ("skb", [P, 2, 256], F32), ("svb", [P, 2, 256], F32), ("q_all", [P, D], F32),
            ("sprod", [P, S], F32), ("sprob", [HEADS, 452], F32), ("sprob_t", [P, 5, HEADS], F32),
            ("sbias", [HEADS, NKA + NKB], F32), ("ssink", [HEADS, 1], F32), ("sc", [P, 5, HEADS], F32),
            ("srow", [HEADS, 16], F32), ("ysm", [P, KT, NB], F32), ("ystmp", [P, KT, NB], F32)])
        f_in, f_out, gf_row = phase([("f_in", [P, 3, D], F32), ("f_out", [P, 2, D], F32), ("gf_row", [P, D], F32)])

        prob_of = [prob[:, 0:1792].rearrange("p (h n) -> p h n", h=2),
                   prob[:, 1792:3840].rearrange("p (h n) -> p h n", h=2)]
        pairs = [("A", j) for j in range(PAIRS)] + [("B", j) for j in range(PAIRS)]
        NT = NZ + KT

        def chunks_of(kind):
            return CHUNKS_A if kind == "A" else CHUNKS_B

        def steps_of(kind, first):
            return range(len(chunks_of(kind)))

        def nat_groups(kind):
            if kind == "A":
                return [("v", range(0, 4), 0), ("v", range(4, 8), 1), ("k", range(0, 4), 4), ("k", range(4, 8), 8)]
            return [("v", range(0, 4), 0), ("v", range(4, 8), 1), ("k", range(7, 8), 4)]

        def walk(visit):
            for n, (kind, j) in enumerate(pairs):
                for s in range(len(chunks_of(kind))):
                    visit(n, s)
            kind = pairs[-1][0]
            for s in range(len(chunks_of(kind)), len(chunks_of(kind)) + 5):
                visit(len(pairs) - 1, s)

        def both(n, s):
            if n and s < len(chunks_of(pairs[n][0])):
                yield n - 1, s + len(chunks_of(pairs[n - 1][0]))
            yield n, s

        def per_pair(name, kind):
            return {"scored": 2, "biased": 2, "turned": 2, "copied0": 1, "copied1": 1, "summed": 1}.get(name, 0) * len(chunks_of(kind)) \
                or {"shifted": QB, "exped": 2 * QB, "scaled": 2 * QB, "y_gated": 2, "nat_turned": len(nat_groups(kind)),
                    "nat_copied": len(nat_groups(kind))}[name]

        def pair_wait(eng, name, n, local):
            if n >= 0:
                kind, j = pairs[n]
                eng.wait_ge(sem(kind + name), per_pair(name, kind) * j + local)

        def buffer_wait(eng, name, n, local, back_all):
            if local > 0:
                pair_wait(eng, name, n, local)
            elif n > 0:
                pair_wait(eng, name, n - 1, per_pair(name, pairs[n - 1][0]) + local)

        block = ctx.enter_context(nc.Block())

        @block.sync
        def _(sp):
            sp.dma_start(ident[:], a["c_ident"]).then_inc(sem("consts"), 16)
            sp.dma_start(g_row[:], bcast_rows(a["g_mix"][0:1, :], P)).then_inc(sem("consts"), 16)
            for i, (r0, n) in enumerate(ROW_TILES):
                if i >= 2:
                    sp.wait_ge(sem("x_normed"), i - 1)
                src = x_p[r0:r0 + n, :] if i < 8 else x_s
                sp.dma_start(x_in[0:n, i % 2, :], src).then_inc(sem(f"x_loaded{i % 2}"), 16)
            with sp.Fori(0, NZ // 2) as it:
                for par in range(2):
                    sp.wait_ge(sem("lo_ready"), it * 2 + par + 1)
                    sp.dma_start(w_raw[:, par], w_in[:, :, bass.ds(it * (2 * P) + par * P, P)]).then_inc(sem(f"w_loaded{par}"), 16)
            sp.wait_ge(sem("produced"), 3 * (2 + NZ))
            sp.wait_ge(sem("z_stored0"), 16 * (NZ // 2 + 1))
            sp.wait_ge(sem("z_stored1"), 16 * (NZ // 2 + 1))
            sp.dma_start(negd[:], a["c_negd"]).then_inc(sem("consts3"), 16)
            sp.dma_start(mask[:], a["c_logc"]).then_inc(sem("consts3"), 16)
            sp.dma_start(slope[:], a["c_slope"]).then_inc(sem("consts3"), 16)
            sp.dma_start(sink[:], bcast_rows(a["sinks"][0:1, :], P)).then_inc(sem("consts3"), 16)
            for n, (kind, j) in enumerate(pairs):
                par = j % 2
                if n >= 2:
                    pk, pj = pairs[n - 2]
                    sp.wait_ge(sem(pk + "y_gated"), 2 * (pj + 1))
                if n >= 1:
                    pk, pj = pairs[n - 1]
                    sp.wait_ge(sem(pk + "nat_turned"), len(nat_groups(pk)) * pj + 2)
                if kind == "A":
                    sp.dma_start(zv[:], z_dram[ZVA + j, :, 0:S]).then_inc(sem("Av_loaded"), 16)
                    sp.dma_start(zq[:, par], z_dram[ZQA + j, :, 0:S]).then_inc(sem(f"Az_loaded{par}"), 16)
                    sp.dma_start(zk[:, par], z_dram[ZKA + j, :, 0:S]).then_inc(sem(f"Az_loaded{par}"), 16)
                    sp.dma_start(zg[:, par], z_dram[ZGA + j, :, 0:S]).then_inc(sem(f"Az_loaded{par}"), 16)
                else:
                    g = j // 2
                    half = slice(HD * (g % 2), HD * (g % 2) + HD)
                    for d in (0, HD):
                        sp.dma_start(zv[d:d + HD, :], z_dram[ZVB + g // 2, half, 0:S]).then_inc(sem("Bv_loaded"), 16)
                    sp.dma_start(zq[:, par], z_dram[ZQB + j, :, 0:S]).then_inc(sem(f"Bz_loaded{par}"), 16)
                    for d in (0, HD):
                        sp.dma_start(zk[d:d + HD, par, :], z_dram[ZKB + g // 2, half, 0:S]).then_inc(sem(f"Bz_loaded{par}"), 16)
                    sp.dma_start(zg[:, par], z_dram[ZGB + j, :, 0:S]).then_inc(sem(f"Bz_loaded{par}"), 16)
                if kind == "B" and j == 0:
                    sp.wait_ge(sem("bias_built"), 2 * PAIRS)
                    sp.dma_start(mask[:, S - 256:S], a["c_band"]).then_inc(sem("consts3"), 16)

            sp.wait_ge(sem("Bv_stored"), 16 * 4)
            sp.wait_ge(sem("Bk_stored"), 16 * 4)
            sp.wait_ge(sem("Ak_stored"), 16 * 16)
            sp.wait_ge(sem("Av_stored"), 16 * 8)
            sp.wait_ge(sem("y_split"), 2 * len(pairs))
            sp.dma_start(zst[:], z_dram[:, :, S:R].rearrange("t p n -> p t n")).then_inc(sem("s_consts"), 16)
            sp.dma_start(sbias[:], a["c_sbias"]).then_inc(sem("s_consts"), 16)
            sp.dma_start(ssink[:], a["sinks"].rearrange("a h -> h a")).then_inc(sem("s_consts"), 16)
            sp.wait_ge(sem("s_rows"), 16 * 6)
            for b in range(NB):
                if b >= 1:
                    sp.wait_ge(sem("s_scored"), b)
                for t, (r0, step, n) in enumerate(SETS):
                    sp.dma_start(sk[0:n, t, :], a["cache_a_k"][0, b, r0:r0 + step * (n - 1) + 1:step].rearrange("r h d -> r (h d)")).then_inc(sem("sk_loaded"), 16)
                sp.dma_start(sk[96:97, MID, :], ak_s[0, b].rearrange("t h d -> t (h d)")).then_inc(sem("sk_loaded"), 16)
                sp.dma_start(skb[:, 0, :], a["cache_b_k"][0, b].rearrange("r h d -> r (h d)")).then_inc(sem("sk_loaded"), 16)
                sp.dma_start(skb[0:1, 1, :], bk_s[0, b].rearrange("t h d -> t (h d)")).then_inc(sem("sk_loaded"), 16)
                sp.dma_start(q_all[:], bcast_rows(q_dram[b:b + 1, :], P)).then_inc(sem("sk_loaded"), 16)
                if b >= 1:
                    sp.wait_ge(sem("s_pv"), b)
                for t, (r0, step, n) in enumerate(SETS):
                    sp.dma_start(sv[0:n, t, :], a["cache_a_v"][0, b, r0:r0 + step * (n - 1) + 1:step].rearrange("r h d -> r (h d)")).then_inc(sem("sv_loaded"), 16)
                sp.dma_start(sv[96:97, MID, :], av_s[0, b].rearrange("t h d -> t (h d)")).then_inc(sem("sv_loaded"), 16)
                sp.dma_start(svb[:, 0, :], a["cache_b_v"][0, b].rearrange("r h d -> r (h d)")).then_inc(sem("sv_loaded"), 16)
                sp.dma_start(svb[0:1, 1, :], bv_s[0, b].rearrange("t h d -> t (h d)")).then_inc(sem("sv_loaded"), 16)

            sp.wait_ge(sem("s_split"), 2)
            with sp.Fori(0, KT // 2) as it:
                for par in range(2):
                    sp.wait_ge(sem("lo_ready"), it * 2 + (NZ + par + 1))
                    sp.dma_start(w_raw[:, par], w_out[:, :, bass.ds(it * (2 * P) + par * P, P)]).then_inc(sem(f"w_loaded{par}"), 16)
                    sp.wait_ge(sem("produced"), 3 * (it * 2 + (NZ + 1 + par)))
                    cols = bass.ds(it * (2 * P) + par * P, P)
                    for t in range(2):
                        q0 = T3 * t
                        sp.dma_start(x_cols[:, par, 3 * t:3 * t + 2, :], x_p[q0:q0 + 256, cols].rearrange("(c p) n -> p c n", p=P)).then_inc(sem(f"xc_loaded{par}"), 16)
                        sp.dma_start(x_cols[0:88, par, 3 * t + 2, :], x_p[q0 + 256:q0 + 344, cols]).then_inc(sem(f"xc_loaded{par}"), 16)
                    sp.dma_start(x_cols[:, par, 6:8, :], x_p[688:944, cols].rearrange("(c p) n -> p c n", p=P)).then_inc(sem(f"xc_loaded{par}"), 16)
                    sp.dma_start(x_cols[0:80, par, 8, :], x_p[944:1024, cols]).then_inc(sem(f"xc_loaded{par}"), 16)
                    sp.dma_start(x_cols[80:88, par, 8, :], x_s[:, cols]).then_inc(sem(f"xc_loaded{par}"), 16)

            sp.wait_ge(sem("produced"), 3 * (2 + NT))
            sp.wait_ge(sem("z_stored0"), 16 * (NT // 2 + 1))
            sp.wait_ge(sem("z_stored1"), 16 * (NT // 2 + 1))
            sp.wait_ge(sem("h_summed"), KT)
            sp.dma_start(gcol[:], a["g_ple"].rearrange("a (k p) -> p (a k)", p=P), allow_slow_non_contiguous=True).then_inc(sem("gcol_loaded"), 16)
            for i, (r0, n) in enumerate(ROW_TILES):
                if i >= 2:
                    sp.wait_ge(sem("p_turned"), i - 1)
                src = p_p[r0:r0 + n, :] if i < 8 else p_s
                sp.dma_start(y_nat[0:n, i % 2, 0:2, :].rearrange("p c n -> p (c n)"), src).then_inc(sem(f"p_loaded{i % 2}"), 16)
            for k in range(KT):
                if k >= 2:
                    sp.wait_ge(sem("h_split"), k - 1)
                sp.dma_start(h_stage[:, k % 2, :], h_dram[k]).then_inc(sem(f"h_loaded{k % 2}"), 16)
            sp.wait_ge(sem("h_split"), KT)

            def load_u(n):
                if n:
                    sp.wait_ge(sem("u_lo_ready"), n)
                sp.dma_start(u_raw[:, 0:KT, :], w_pg[:, :, n * P:(n + 1) * P]).then_inc(sem("u_loaded"), 16)
                sp.dma_start(u_raw[:, KT:, :], w_ple[:, :, n * P:(n + 1) * P]).then_inc(sem("u_loaded"), 16)

            load_u(0)
            for n in range(KT):
                if n + 1 < KT:
                    load_u(n + 1)
                for t in range(3):
                    u = 3 * n + t
                    if u >= 2:
                        sp.wait_ge(sem("h_added"), u - 1)
                    sp.dma_start(h_in[:, u % 2, :], h_dram[n, :, T3 * t:T3 * (t + 1)]).then_inc(sem(f"hin_loaded{u % 2}"), 16)
            sp.wait_ge(sem("u_produced"), 3 * KT)
            for par in range(2):
                sp.wait_ge(sem(f"y_stored{par}"), 16 * 3 * KT)
            sp.dma_start(gf_row[:], bcast_rows(a["g_final"].rearrange("(a d) -> a d", a=1), P)).then_inc(sem("gf_loaded"), 16)
            for i, (r0, n) in enumerate(ROW_TILES):
                if i >= 3:
                    sp.wait_ge(sem("f_scaled"), i - 2)
                sp.dma_start(f_in[0:n, i % 3, :], y_dram[r0:r0 + n, :]).then_inc(sem(f"f_loaded{i % 3}"), 16)
            sp.wait_ge(sem("out_stored0"), 16 * 5)
            sp.wait_ge(sem("out_stored1"), 16 * 4)

        @block.gpsimd
        def _(pool):
            def visit(n_, s_):
                for n, s in both(n_, s_):
                    kind, j = pairs[n]
                    ch, turn = chunks_of(kind), turn_step(chunks_of(kind))
                    groups = nat_groups(kind)
                    for gi, (what, blks, at) in enumerate(groups):
                        if at != s or (what == "v" and gi == 0):
                            continue
                        if kind == "A":
                            pool.wait_ge(sem("Anat_copied"), 4 * j + gi + 1)
                            if what == "v":
                                pool.dma_start(av_p[0, 0, :, 2 * j:2 * j + 2, :].rearrange("(c p) h d -> p c (h d)", p=P),
                                               v_nat[:, j % 2]).then_inc(sem("Av_stored"), 16)
                            else:
                                pool.dma_start(ak_p[0, 0, blks[0] * P:(blks[-1] + 1) * P, 2 * j:2 * j + 2, :].rearrange("(c p) h d -> p c (h d)", p=P),
                                               k_nat[:]).then_inc(sem("Ak_stored"), 16)
                        elif j % 2 == 0:
                            pool.wait_ge(sem("Bnat_copied"), 3 * j + gi + 1)
                            if what == "v":
                                pool.dma_start(bv_p[0, 0, :, j // 2, :], v_nat[:, j % 2, 7, 0:HD]).then_inc(sem("Bv_stored"), 16)
                            else:
                                pool.dma_start(bk_p[0, 0, :, j // 2, :], k_nat[:, 0, 0:HD]).then_inc(sem("Bk_stored"), 16)
                    for half in range(2):
                        if turn[last_chunk(ch, 4 * half + 3)] + 1 == s:
                            pool.wait_ge(sem(kind + "y_gated"), 2 * j + half + 1)
                            dst = slice(512 * half, 512 * half + 512)
                            pool.tensor_copy(act_hi[:, n, dst], yt[:]).then_inc(sem("y_hi"), 1)
                            pool.wait_ge(sem("y_hi"), 2 * n + half + 1)
                            pool.tensor_tensor(act_lo[:, n, dst], yt[:], hi32[:, n, dst], ALU.subtract).then_inc(sem("y_split"), 1)
            walk(visit)

            rows = lambda ap: ap.rearrange("l b t h d -> (l b t) (h d)")
            pool.wait_ge(sem("s_nat"), 9)
            zr = zn[:].rearrange("p c n -> p (c n)")
            pool.dma_start(q_dram[:, 0:S], zr[:, 0:S]).then_inc(sem("s_rows"), 16)
            pool.dma_start(rows(ak_s), zr[:, S:2 * S]).then_inc(sem("s_rows"), 16)
            pool.dma_start(rows(av_s), zr[:, 2 * S:3 * S]).then_inc(sem("s_rows"), 16)
            pool.dma_start(q_dram[:, S:D], zr[:, 3 * S:4 * S]).then_inc(sem("s_rows"), 16)
            pool.dma_start(rows(bk_s), zr[:, 4 * S:4 * S + 256]).then_inc(sem("s_rows"), 16)
            pool.dma_start(rows(bv_s), zr[:, 4 * S + 256:4 * S + 512]).then_inc(sem("s_rows"), 16)

            pool.wait_ge(sem("s_split"), 2)
            pool.memset(ones[:], 1.0).then_inc(sem("ones_set"), 1)
            pool.memset(acc[:], 0.0).then_inc(sem("acc_set"), 1)
            pool.sem_inc(sem("h_squared"), 2)
            pool.wait_ge(sem("acc_set"), 1)
            with pool.Fori(0, KT // 2) as it:
                for par in range(2):
                    pool.wait_ge(sem("bank_free"), it * 6 + (6 + 3 * NZ + 3 * par + 3))
                    pool.tensor_tensor(sq[:], stage[:, par], stage[:, par], ALU.mult).then_inc(sem("h_squared"), 1)
                    pool.wait_ge(sem("h_squared"), it * 2 + (par + 3))
                    pool.tensor_tensor(acc[:], acc[:], sq[:], ALU.add).then_inc(sem("h_summed"), 1)
                    pool.wait_ge(sem("h_summed"), it * 2 + par + 1)

            for n in range(KT):
                for t in range(3):
                    u = 3 * n + t
                    pool.wait_ge(sem("y_copied"), u + 1)
                    q0 = T3 * t
                    pool.dma_start(y_dram[q0:q0 + 256, n * P:(n + 1) * P].rearrange("(c p) n -> p c n", p=P), y_nat[:, u % 2, 0:2, :]).then_inc(sem(f"y_stored{u % 2}"), 16)
                    pool.dma_start(y_dram[q0 + 256:q0 + T3, n * P:(n + 1) * P], y_nat[0:88, u % 2, 2, :]).then_inc(sem(f"y_stored{u % 2}"), 16)
            for i, (r0, n) in enumerate(ROW_TILES):
                pool.wait_ge(sem("f_scaled"), i + 1)
                dst = yp[r0:r0 + n, :] if i < 8 else ys
                pool.dma_start(dst, f_out[0:n, i % 2, :]).then_inc(sem(f"out_stored{i % 2}"), 16)

        @block.tensor
        def _(pe):
            pe.wait_ge(sem("consts"), 32)
            for i, (r0, n) in enumerate(ROW_TILES):
                pe.wait_ge(sem("x_normed"), i + 1)
                for q in range(4):
                    u = 4 * i + q
                    if u >= 8:
                        pe.wait_ge(sem("x_lo"), u - 7)
                    for m in range(4):
                        k = 4 * q + m
                        mm = pe.transpose(psum[:, u % 8, n * m:n * m + n], x_n[0:n, i % 2, k * P:(k + 1) * P], ident[0:n, 0:n])
                    mm.then_inc(sem("x_turned"), 1)

            def product(bank, par, hi_w, lo_w, hi_a, lo_a, t, tiles, close):
                rows = slice(T3 * t, T3 * (t + 1))
                for k in range(tiles):
                    pe.matmul(psum[:, bank, 0:T3], hi_w(k), hi_a[:, k, rows], start=(k == 0), stop=False, skip_group_check=True)
                    pe.matmul(psum[:, bank, 0:T3], hi_w(k), lo_a[:, k, rows], start=False, stop=False, skip_group_check=True)
                    mm = pe.matmul(psum[:, bank, 0:T3], lo_w(k), hi_a[:, k, rows], start=False,
                                   stop=(close and k == tiles - 1), skip_group_check=True)
                return mm

            pe.sem_inc(sem("produced"), 6)
            pe.wait_ge(sem("x_lo"), 4 * len(ROW_TILES))
            with pe.Fori(0, NZ // 2) as it:
                for par in range(2):
                    pe.wait_ge(sem("lo_ready"), it * 2 + (par + 3))
                    for t in range(3):
                        pe.wait_ge(sem("bank_free"), it * 6 + (3 * par + t + 1))
                        mm = product(3 * par + t, par, lambda k: w_hi[:, par, k, :], lambda k: w_lo[:, par, k, :], act_hi, act_lo, t, KT, True)
                        mm.then_inc(sem("produced"), 1)

            def visit(n_, s_):
                kind, j = pairs[n_]
                ch = chunks_of(kind)
                c = s_
                if c == 0:
                    pe.wait_ge(sem(f"{kind}z_loaded{j % 2}"), 16 * (3 if kind == "A" else 4) * (j // 2 + 1))
                if c < len(ch):
                    b, k0, nk = ch[c]
                    for h in range(2):
                        buffer_wait(pe, "biased", n_, 2 * (c - 2) + h + 1, None)
                        pe.matmul(psum[:, 2 * h + c % 2, 0:nk], zq[HD * h:HD * h + HD, j % 2, b * BLK:(b + 1) * BLK],
                                  zk[HD * h:HD * h + HD, j % 2, k0:k0 + nk], start=True, stop=True).then_inc(sem(kind + "scored"), 1)
                for n, s in both(n_, s_):
                    kind, j = pairs[n]
                    ch = chunks_of(kind)
                    turn = turn_step(ch)
                    for c, (b, k0, nk) in enumerate(ch):
                        if turn[c] == s:
                            for h in range(2):
                                pair_wait(pe, "scaled", n, 2 * b + h + 1)
                                buffer_wait(pe, f"copied{h}", n, c, None)
                                for x in range(nk // P):
                                    mm = pe.transpose(psum[:, 4 + h, x * P:(x + 1) * P], prob_of[b % 2][:, h, k0 - off(kind, b) + x * P:k0 - off(kind, b) + (x + 1) * P], ident[:])
                                mm.then_inc(sem(kind + "turned"), 1)
                    for c, (b, k0, nk) in enumerate(ch):
                        if turn[c] + 1 == s:
                            if b % 4 == 0 and c == last_chunk(ch, b - 1) + 1 if b else c == 0:
                                buffer_wait(pe, "y_gated", n, b // 4, None)
                            if c == 0:
                                pair_wait(pe, "nat_copied", n, 1)
                            if b == 4:
                                pair_wait(pe, "nat_copied", n, 2)
                            first = k0 == off(kind, b)
                            last = k0 + nk == (b + 1) * BLK
                            for h in range(2):
                                pair_wait(pe, f"copied{h}", n, c + 1)
                                for x in range(nk // P):
                                    mm = pe.matmul(psum[HD * h:HD * h + HD, 6, (b % 4) * P:(b % 4 + 1) * P],
                                                   v_nat[:, j % 2, k0 // P + x, HD * h:HD * h + HD], prob_t[:, h, x * P:(x + 1) * P],
                                                   start=(b % 4 == 0 and first and x == 0), stop=(last and x == nk // P - 1), skip_group_check=True)
                            mm.then_inc(sem(kind + "summed"), 1)
                kind, j = pairs[n_]
                for gi, (what, blks, at) in enumerate(nat_groups(kind)):
                    if at == s_:
                        if gi == 0:
                            pe.wait_ge(sem(kind + "v_loaded"), 16 * (1 if kind == "A" else 2) * (j + 1))
                        buffer_wait(pe, "nat_copied", n_, gi, None)
                        for x, blk in enumerate(blks):
                            src = zv[:, blk * P:(blk + 1) * P] if what == "v" else zk[:, j % 2, blk * P:(blk + 1) * P]
                            mm = pe.transpose(psum[:, 7, x * P:(x + 1) * P], src, ident[:])
                        mm.then_inc(sem(kind + "nat_turned"), 1)
            walk(visit)

            pe.wait_ge(sem("s_consts"), 48)
            for g in range(9):
                if g >= 2:
                    pe.wait_ge(sem("s_nat"), g - 1)
                for m in range(4):
                    mm = pe.transpose(psum[0:NB, g % 2, m * P:(m + 1) * P], zst[:, S_TILES[4 * g + m], :], ident[:])
                mm.then_inc(sem("s_turned"), 1)
            for b in range(NB):
                pe.wait_ge(sem("s_scored"), b + 1)
                if b >= 1:
                    pe.wait_ge(sem("s_biased"), 2 * b)
                for t in range(3):
                    pe.transpose(psum[0:HEADS, 2, SCOL[t]:SCOL[t] + SROWS[t]], sc[0:SROWS[t], t, :], ident[0:SROWS[t], 0:SROWS[t]])
                pe.transpose(psum[0:HEADS, 3, 0:128], sc[:, 3, :], ident[:])
                pe.transpose(psum[0:HEADS, 3, 128:129], sc[0:1, 4, :], ident[0:1, 0:1]).then_inc(sem("s_rowed"), 1)
                pe.wait_ge(sem("s_scaled"), 2 * (b + 1))
                if b >= 1:
                    pe.wait_ge(sem("s_pcopied"), 5 * b)
                for t, (c0, n) in enumerate(SPIECES):
                    mm = pe.transpose(psum[0:n, 4, 16 * t:16 * t + 16], sprob[:, c0:c0 + n], ident[0:HEADS, 0:HEADS])
                mm.then_inc(sem("s_pturned"), 1)
                pe.wait_ge(sem("s_pcopied"), 5 * (b + 1))
                pe.wait_ge(sem("sv_loaded"), 16 * 6 * (b + 1))
                if b >= 1:
                    pe.wait_ge(sem("s_ycopied"), 4 * b)
                for j in range(PAIRS):
                    for t in range(3):
                        pe.matmul(psum[:, 5, 2 * j:2 * j + 2], sv[0:SROWS[t], t, P * j:P * (j + 1)],
                                  sprob_t[0:SROWS[t], t, 2 * j:2 * j + 2], start=(t == 0), stop=(t == 2))
                for g in range(KVH):
                    pe.matmul(psum[0:HD, 6, 4 * g:4 * g + 4], svb[:, 0, HD * g:HD * (g + 1)], sprob_t[:, 3, 4 * g:4 * g + 4], start=True, stop=False)
                    mm = pe.matmul(psum[0:HD, 6, 4 * g:4 * g + 4], svb[0:1, 1, HD * g:HD * (g + 1)], sprob_t[0:1, 4, 4 * g:4 * g + 4], start=False, stop=True)
                mm.then_inc(sem("s_pv"), 1)

            pe.wait_ge(sem("s_split"), 2)
            with pe.Fori(0, KT // 2) as it:
                for par in range(2):
                    pe.wait_ge(sem("lo_ready"), it * 2 + (NZ + par + 3))
                    for t in range(3):
                        bank = 3 * par + t
                        pe.wait_ge(sem("bank_free"), it * 6 + (3 * NZ + 3 * par + t + 1))
                        product(bank, par, lambda k: w_hi[:, par, k, :], lambda k: w_lo[:, par, k, :], act_hi, act_lo, t, KT, False)
                        if t == 0:
                            pe.wait_ge(sem(f"xc_loaded{par}"), it * 112 + 112)
                        for x, (c0, n) in enumerate(PIECES[t]):
                            mm = pe.matmul(psum[:, bank, c0:c0 + n], x_cols[0:n, par, 3 * t + x, :], ident[0:n, 0:n], start=False, stop=(x == 2), skip_group_check=True)
                        mm.then_inc(sem("produced"), 1)

            pe.wait_ge(sem("h_summed"), KT)
            pe.wait_ge(sem("bank_free"), 3 * NT + 6)
            for t in range(3):
                mm = pe.matmul(psum[:, t, 0:T3], ones[:], acc[:, T3 * t:T3 * (t + 1)], start=True, stop=True)
            mm.then_inc(sem("h_meaned"), 1)
            for i, (r0, n) in enumerate(ROW_TILES):
                pe.wait_ge(sem(f"p_loaded{i % 2}"), 16 * (i // 2 + 1))
                if i >= 2:
                    pe.wait_ge(sem("p_lo"), i - 1)
                for m in range(2):
                    mm = pe.transpose(psum[:, 6 + i % 2, n * m:n * m + n], y_nat[0:n, i % 2, m, :], ident[0:n, 0:n])
                mm.then_inc(sem("p_turned"), 1)
            pe.wait_ge(sem("p_lo"), len(ROW_TILES))
            pe.wait_ge(sem("h_split"), KT)
            pe.wait_ge(sem("h_rooted"), 3)

            def y_turn(u):
                pe.wait_ge(sem("h_added"), u + 1)
                if u >= 2:
                    pe.wait_ge(sem("y_copied"), u - 1)
                for x, (c0, n) in enumerate(PIECES[u % 3]):
                    mm = pe.transpose(psum[0:n, 6 + u % 2, x * P:(x + 1) * P], t_y[:, u % 2, c0:c0 + n], ident[:])
                mm.then_inc(sem("y_turned"), 1)

            for n in range(KT):
                par = n % 2
                pe.wait_ge(sem("u_lo_ready"), n + 1)
                for t in range(3):
                    u = 3 * n + t
                    if u >= 3:
                        pe.wait_ge(sem("p_read"), u - 2)
                    product(t, par, lambda k: u_hi[:, par, k, :], lambda k: u_lo[:, par, k, :], act_hi, act_lo, t, KT, True)
                    mm = product(3 + t, par, lambda k: u_hi[:, par, KT + k, :], lambda k: u_lo[:, par, KT + k, :], pt_hi, pt_lo, t, 2, True)
                    mm.then_inc(sem("u_produced"), 1)
                    if u >= 1:
                        y_turn(u - 1)
            y_turn(3 * KT - 1)

        @block.scalar
        def _(act):
            def x_hi_copies(i):
                r0, n = ROW_TILES[i]
                for q in range(4):
                    u = 4 * i + q
                    act.wait_ge(sem("x_turned"), u + 1)
                    act.activation(act_hi[:, 4 * q:4 * q + 4, r0:r0 + n], psum[:, u % 8, 0:4 * n].rearrange("p (m r) -> p m r", m=4), ACT.Copy).then_inc(sem("x_hi"), 1)
            for i, (r0, n) in enumerate(ROW_TILES):
                act.wait_ge(sem(f"x_loaded{i % 2}"), 16 * (i // 2 + 1))
                if i >= 2:
                    act.wait_ge(sem("x_turned"), 4 * (i - 1))
                act.activation(x_n[0:n, i % 2, :], x_in[0:n, i % 2, :], ACT.Square, accum_out=small[0:n, i:i + 1]).then_inc(sem("x_squared"), 1)
                act.wait_ge(sem("x_meaned"), i + 1)
                act.activation(small[0:n, 9 + i:10 + i], small[0:n, i:i + 1], ACT.Sqrt).then_inc(sem("x_rooted"), 1)
                if i >= 1:
                    x_hi_copies(i - 1)
            x_hi_copies(8)
            act.wait_ge(sem("x_hi"), 36)
            act.wait_ge(sem("x_lo"), 36)
            act.sem_inc(sem("bank_free"), 6)
            act.sem_inc(sem("z_stored0"), 16)
            act.sem_inc(sem("z_stored1"), 16)
            for func, first, tiles in ((ACT.Copy, 0, 24), (ACT.Silu, ZGA, 8), (ACT.Copy, ZQB, 12), (ACT.Silu, ZGB, 8)):
                with act.Fori(0, tiles // 2) as it:
                    for par in range(2):
                        act.wait_ge(sem(f"z_stored{par}"), it * 16 + 16 * (first // 2 + 1))
                        for t in range(3):
                            act.wait_ge(sem("produced"), it * 6 + (3 * first + 3 * par + t + 7))
                            act.activation(stage[:, par, T3 * t:T3 * (t + 1)], psum[:, 3 * par + t, 0:T3], func).then_inc(sem("bank_free"), 1)
                        act.wait_ge(sem("bank_free"), it * 6 + (3 * first + 3 * par + 9))
                        act.dma_start(z_dram[it * 2 + (first + par)], stage[:, par]).then_inc(sem(f"z_stored{par}"), 16)

            def visit(n_, s_):
                for n, s in both(n_, s_):
                    kind, j = pairs[n]
                    ch, turn = chunks_of(kind), turn_step(chunks_of(kind))
                    for c, (b, k0, nk) in enumerate(ch):
                        if turn[c] == s:
                            pair_wait(act, "turned", n, 2 * c + 1)
                            buffer_wait(act, "summed", n, c, None)
                            act.activation(prob_t[:, 0, 0:nk], psum[:, 4, 0:nk], ACT.Copy).then_inc(sem(kind + "copied0"), 1)
                    if s < len(ch) and s == last_chunk(ch, ch[s][0]):
                        b = ch[s][0]
                        w = (b + 1) * BLK - off(kind, b)
                        pair_wait(act, "shifted", n, b + 1)
                        m = mx[:, b % 2]
                        if kind == "B":
                            for h in range(2):
                                act.activation(m[:, 10 + h:11 + h], sink[:, 2 * j + h:2 * j + h + 1], ACT.Exp, bias=m[:, 4 + h:5 + h])
                        for h in range(2):
                            pr = prob_of[b % 2][:, h, 0:w]
                            act.activation(pr, pr, ACT.Exp, bias=m[:, 4 + h:5 + h], accum_out=m[:, 6 + h:7 + h]).then_inc(sem(kind + "exped"), 1)
                    for gi, (what, blks, at) in enumerate(nat_groups(kind)):
                        if at == s:
                            pair_wait(act, "nat_turned", n, gi + 1)
                            w = len(blks) * P
                            if what == "v":
                                if n >= 2 and gi == 0:
                                    pair_wait(act, "y_gated", n - 2, 2)
                                    pk, pj = pairs[n - 2]
                                    act.wait_ge(sem(pk + "v_stored"), 16 * (pj + 1 if pk == "A" else pj // 2 + 1))
                                dst = v_nat[:, j % 2, blks[0]:blks[-1] + 1, :].rearrange("p c m -> p (c m)")
                            else:
                                count = (2 * j + gi - 2 if kind == "A" else (j + 1) // 2)
                                if kind == "B":
                                    act.wait_ge(sem("Ak_stored"), 16 * 16)
                                if count:
                                    act.wait_ge(sem(kind + "k_stored"), 16 * count)
                                dst = k_nat[:, 0:len(blks), :].rearrange("p c m -> p (c m)")
                            act.activation(dst, psum[:, 7, 0:w], ACT.Copy).then_inc(sem(kind + "nat_copied"), 1)
            act.wait_ge(sem("consts3"), 64)
            walk(visit)

            for g in range(9):
                act.wait_ge(sem("s_turned"), g + 1)
                act.activation(zn[:, 4 * g:4 * g + 4, :].rearrange("p c m -> p (c m)"), psum[0:NB, g % 2, :], ACT.Copy).then_inc(sem("s_nat"), 1)
            for b in range(NB):
                act.wait_ge(sem("s_shifted"), 2 * (b + 1))
                act.activation(sprob[:, 0:NKA], sprob[:, 0:NKA], ACT.Exp, bias=srow[:, 3:4], accum_out=srow[:, 5:6]).then_inc(sem("s_exped"), 1)
                act.activation(sprob[:, NKA:NKA + NKB], sprob[:, NKA:NKA + NKB], ACT.Exp, bias=srow[:, 4:5], accum_out=srow[:, 6:7]).then_inc(sem("s_exped"), 1)
                act.activation(srow[:, 7:8], ssink[:], ACT.Exp, bias=srow[:, 4:5]).then_inc(sem("s_exped"), 1)

            with act.Fori(0, KT // 2) as it:
                for par in range(2):
                    act.wait_ge(sem(f"z_stored{par}"), it * 16 + 16 * (NZ // 2 + 1))
                    act.wait_ge(sem("h_squared"), it * 2 + (par + 1))
                    for t in range(3):
                        act.wait_ge(sem("produced"), it * 6 + (3 * NZ + 3 * par + t + 7))
                        act.activation(stage[:, par, T3 * t:T3 * (t + 1)], psum[:, 3 * par + t, 0:T3], ACT.Copy).then_inc(sem("bank_free"), 1)
                    act.wait_ge(sem("bank_free"), it * 6 + (3 * NZ + 3 * par + 9))
                    act.dma_start(h_dram[it * 2 + par], stage[:, par]).then_inc(sem(f"z_stored{par}"), 16)

            for t in range(3):
                act.wait_ge(sem("h_eps"), t + 1)
                act.activation(acc[:, T3 * t:T3 * (t + 1)], acc[:, T3 * t:T3 * (t + 1)], ACT.Sqrt).then_inc(sem("h_sqrt"), 1)
            for i, (r0, n) in enumerate(ROW_TILES):
                act.wait_ge(sem("p_turned"), i + 1)
                act.activation(pt_hi[:, :, r0:r0 + n], psum[:, 6 + i % 2, 0:2 * n].rearrange("p (m r) -> p m r", m=2), ACT.Copy).then_inc(sem("p_hi"), 1)
            act.wait_ge(sem("gcol_loaded"), 16)
            for k in range(KT):
                act.wait_ge(sem(f"h_loaded{k % 2}"), 16 * (k // 2 + 1))
                act.activation(act_hi[:, k, :], h_stage[:, k % 2, :], ACT.Copy, scale=gcol[:, k:k + 1]).then_inc(sem("h_hi"), 1)

            def y_copy(u):
                act.wait_ge(sem("y_turned"), u + 1)
                if u >= 2:
                    act.wait_ge(sem(f"y_stored{u % 2}"), 32 * (u // 2))
                act.activation(y_nat[:, u % 2, 0:2, :], psum[:, 6 + u % 2, 0:256].rearrange("p (c n) -> p c n", c=2), ACT.Copy)
                act.activation(y_nat[0:88, u % 2, 2, :], psum[0:88, 6 + u % 2, 256:384], ACT.Copy).then_inc(sem("y_copied"), 1)
            for u in range(3 * KT):
                act.wait_ge(sem("g_scaled"), u + 1)
                act.activation(t_gate[:, u % 2, :], t_gate[:, u % 2, :], ACT.Sigmoid).then_inc(sem("gated"), 1)
                if u >= 2:
                    y_copy(u - 2)
            y_copy(3 * KT - 2)
            y_copy(3 * KT - 1)

            for i, (r0, n) in enumerate(ROW_TILES):
                act.wait_ge(sem(f"f_loaded{i % 3}"), 16 * (i // 3 + 1))
                if i >= 2:
                    act.wait_ge(sem(f"out_stored{i % 2}"), 16 * (i // 2))
                act.activation(f_out[0:n, i % 2, :], f_in[0:n, i % 3, :], ACT.Square, accum_out=small[0:n, 32 + i:33 + i]).then_inc(sem("f_squared"), 1)
                act.wait_ge(sem("f_meaned"), i + 1)
                act.activation(small[0:n, 41 + i:42 + i], small[0:n, 32 + i:33 + i], ACT.Sqrt).then_inc(sem("f_rooted"), 1)

        @block.vector
        def _(dve):
            done = [0]

            def chain(ins):
                done[0] += 1
                ins.then_inc(sem("dve_chain"), 1)
                dve.wait_ge(sem("dve_chain"), done[0])

            dve.sem_inc(sem("lo_ready"), 2)
            def x_lo_parts(i):
                r0, n = ROW_TILES[i]
                for q in range(4):
                    u = 4 * i + q
                    dve.wait_ge(sem("x_hi"), u + 1)
                    dve.tensor_tensor(act_lo[:, 4 * q:4 * q + 4, r0:r0 + n], psum[:, u % 8, 0:4 * n].rearrange("p (m r) -> p m r", m=4),
                                      hi32[:, 4 * q:4 * q + 4, r0:r0 + n], ALU.subtract).then_inc(sem("x_lo"), 1)
            dve.wait_ge(sem("consts"), 32)
            for i, (r0, n) in enumerate(ROW_TILES):
                dve.wait_ge(sem("x_squared"), i + 1)
                dve.tensor_scalar(small[0:n, i:i + 1], small[0:n, i:i + 1], 1.0 / D, EPS, ALU.mult, ALU.add).then_inc(sem("x_meaned"), 1)
                dve.wait_ge(sem("x_rooted"), i + 1)
                chain(dve.reciprocal(small[0:n, 18 + i:19 + i], small[0:n, 9 + i:10 + i]))
                dve.scalar_tensor_tensor(x_n[0:n, i % 2, :], x_in[0:n, i % 2, :], small[0:n, 18 + i:19 + i], g_row[0:n, :],
                                         ALU.mult, ALU.mult).then_inc(sem("x_normed"), 1)
                if i >= 1:
                    x_lo_parts(i - 1)
            x_lo_parts(8)

            def split_weights(tiles, first):
                with dve.Fori(0, tiles // 2) as it:
                    for par in range(2):
                        dve.wait_ge(sem(f"w_loaded{par}"), it * 16 + 16 * (first // 2 + 1))
                        dve.wait_ge(sem("produced"), 3 * (it * 2 + (first + par + 1)))
                        dve.tensor_copy(w_hi[:, par], w_raw[:, par]).then_inc(sem("hi_ready"), 1)
                        dve.wait_ge(sem("hi_ready"), it * 2 + (first + par + 1))
                        dve.tensor_tensor(w_lo[:, par], w_raw[:, par], w_hi[:, par].bitcast(F32), ALU.subtract).then_inc(sem("lo_ready"), 1)
            split_weights(NZ, 0)

            def visit(n_, s_):
                for n, s in both(n_, s_):
                    kind, j = pairs[n]
                    ch, turn = chunks_of(kind), turn_step(chunks_of(kind))
                    for half in range(2):
                        if turn[last_chunk(ch, 4 * half + 3)] + 1 == s:
                            pair_wait(dve, "summed", n, last_chunk(ch, 4 * half + 3) + 1)
                            if n or half:
                                dve.wait_ge(sem("y_split"), 2 * n + half)
                            dve.tensor_tensor(yt[:], psum[:, 6, :], zg[:, j % 2, 512 * half:512 * half + 512], ALU.mult).then_inc(sem(kind + "y_gated"), 1)
                    for c, (b, k0, nk) in enumerate(ch):
                        if turn[c] == s:
                            pair_wait(dve, "turned", n, 2 * c + 2)
                            buffer_wait(dve, "summed", n, c, None)
                            dve.tensor_copy(prob_t[:, 1, 0:nk], psum[:, 5, 0:nk]).then_inc(sem(kind + "copied1"), 1)
                    for b in range(QB):
                        if last_chunk(ch, b) + 1 == s:
                            pair_wait(dve, "exped", n, 2 * b + 2)
                            m = mx[:, b % 2]
                            den = m[:, 6:8]
                            if kind == "B":
                                chain(dve.tensor_tensor(m[:, 12:14], m[:, 6:8], m[:, 10:12], ALU.add))
                                den = m[:, 12:14]
                            chain(dve.reciprocal(m[:, 8:10], den))
                            w = (b + 1) * BLK - off(kind, b)
                            for h in range(2):
                                pr = prob_of[b % 2][:, h, 0:w]
                                dve.tensor_scalar(pr, pr, m[:, 8 + h:9 + h], None, ALU.mult).then_inc(sem(kind + "scaled"), 1)
                    if s == 0:
                        if kind == "B":
                            dve.wait_ge(sem("consts3"), 80)
                        w = S if kind == "A" else 2 * BLK
                        for h in range(2):
                            chain(dve.scalar_tensor_tensor(bias[:, h, S - w:S], negd[:, S - w:S], slope[:, 2 * j + h:2 * j + h + 1], mask[:, S - w:S], ALU.mult, ALU.add))
                        dve.sem_inc(sem("bias_built"), 2)
                    if s < len(ch):
                        b, k0, nk = ch[s]
                        m = mx[:, b % 2]
                        part = s - (last_chunk(ch, b - 1) + 1 if b else 0)
                        u0 = k0 - b * BLK + S - BLK
                        for h in range(2):
                            pair_wait(dve, "scored", n, 2 * s + h + 1)
                            if b >= 2:
                                pair_wait(dve, "turned", n, 2 * (last_chunk(ch, b - 2) + 1))
                            elif n:
                                pch = chunks_of(pairs[n - 1][0])
                                pair_wait(dve, "turned", n - 1, 2 * (last_chunk(pch, 6 + b) + 1))
                            dve.tensor_tensor_reduce(prob_of[b % 2][:, h, k0 - off(kind, b):k0 - off(kind, b) + nk], psum[:, 2 * h + s % 2, 0:nk],
                                                     bias[:, h, u0:u0 + nk], SCALE, -3e38, ALU.add, ALU.max, m[:, 2 * part + h:2 * part + h + 1]).then_inc(sem(kind + "biased"), 1)
                        if s == last_chunk(ch, b):
                            pair_wait(dve, "biased", n, 2 * s + 2)
                            if part:
                                chain(dve.tensor_tensor(m[:, 0:2], m[:, 0:2], m[:, 2:4], ALU.max))
                            if kind == "B":
                                chain(dve.tensor_tensor(m[:, 0:2], m[:, 0:2], sink[:, 2 * j:2 * j + 2], ALU.max))
                            dve.tensor_scalar(m[:, 4:6], m[:, 0:2], -1.0, None, ALU.mult).then_inc(sem(kind + "shifted"), 1)
            dve.wait_ge(sem("consts3"), 64)
            walk(visit)

            for b in range(NB):
                dve.wait_ge(sem("sk_loaded"), 16 * 7 * (b + 1))
                if b >= 1:
                    dve.wait_ge(sem("s_rowed"), b)
                for t in range(3):
                    n = SROWS[t]
                    chain(dve.tensor_tensor(sprod[0:n, :], sk[0:n, t, :], q_all[0:n, 0:S], ALU.mult))
                    chain(dve.tensor_reduce(sc[0:n, t, :], sprod[0:n, :].rearrange("p (h d) -> p h d", d=HD), AX.X, ALU.add))
                for t, n in ((0, 128), (1, 1)):
                    kk = skb[0:n, t, :].rearrange("p (g d) -> p g d", d=HD)
                    for g in range(KVH):
                        kg = kk[:, g:g + 1, :].to_broadcast([n, 4, HD])
                        m = dve.tensor_tensor(sprod[0:n, 256 * g:256 * g + 256].rearrange("p (r d) -> p r d", d=HD), kg,
                                              q_all[0:n, S + 256 * g:S + 256 * g + 256].rearrange("p (r d) -> p r d", d=HD), ALU.mult)
                    chain(m)
                    m = dve.tensor_reduce(sc[0:n, 3 + t, :], sprod[0:n, :].rearrange("p (h d) -> p h d", d=HD), AX.X, ALU.add)
                    if t == 0:
                        chain(m)
                m.then_inc(sem("s_scored"), 1)
                dve.wait_ge(sem("s_rowed"), b + 1)
                if b >= 1:
                    dve.wait_ge(sem("s_pturned"), b)
                dve.tensor_tensor_reduce(sprob[:, 0:NKA], psum[0:HEADS, 2, 0:NKA], sbias[:, 0:NKA], SCALE, -3e38, ALU.add, ALU.max, srow[:, 0:1]).then_inc(sem("s_biased"), 1)
                dve.tensor_tensor_reduce(sprob[:, NKA:NKA + NKB], psum[0:HEADS, 3, 0:NKB], sbias[:, NKA:NKA + NKB], SCALE, -3e38, ALU.add, ALU.max, srow[:, 1:2]).then_inc(sem("s_biased"), 1)
                dve.wait_ge(sem("s_biased"), 2 * (b + 1))
                chain(dve.tensor_tensor(srow[:, 2:3], srow[:, 1:2], ssink[:], ALU.max))
                dve.tensor_scalar(srow[:, 3:4], srow[:, 0:1], -1.0, None, ALU.mult).then_inc(sem("s_shifted"), 1)
                dve.tensor_scalar(srow[:, 4:5], srow[:, 2:3], -1.0, None, ALU.mult).then_inc(sem("s_shifted"), 1)
                dve.wait_ge(sem("s_exped"), 3 * (b + 1))
                chain(dve.tensor_tensor(srow[:, 6:7], srow[:, 6:7], srow[:, 7:8], ALU.add))
                chain(dve.reciprocal(srow[:, 9:11], srow[:, 5:7]))
                dve.tensor_scalar(sprob[:, 0:NKA], sprob[:, 0:NKA], srow[:, 9:10], None, ALU.mult).then_inc(sem("s_scaled"), 1)
                dve.tensor_scalar(sprob[:, NKA:NKA + NKB], sprob[:, NKA:NKA + NKB], srow[:, 10:11], None, ALU.mult).then_inc(sem("s_scaled"), 1)
                dve.wait_ge(sem("s_pturned"), b + 1)
                if b >= 1:
                    dve.wait_ge(sem("s_pv"), b)
                for t, (c0, n) in enumerate(SPIECES):
                    dve.tensor_copy(sprob_t[0:n, t, :], psum[0:n, 4, 16 * t:16 * t + 16]).then_inc(sem("s_pcopied"), 1)
                dve.wait_ge(sem("s_pv"), b + 1)
                for h in range(2):
                    half = slice(HD * h, HD * h + HD)
                    dve.tensor_copy(ysm[half, 0:8, b], psum[half, 5, h:16:2]).then_inc(sem("s_ycopied"), 1)
                    dve.tensor_copy(ysm[half, 8:16, b], psum[0:HD, 6, h:16:2]).then_inc(sem("s_ycopied"), 1)
            dve.wait_ge(sem("s_ycopied"), 4 * NB)
            dve.tensor_tensor(ystmp[:, 0:8, :], ysm[:, 0:8, :], zst[:, ZGA:ZGA + 8, :], ALU.mult)
            chain(dve.tensor_tensor(ystmp[:, 8:16, :], ysm[:, 8:16, :], zst[:, ZGB:ZGB + 8, :], ALU.mult))
            chain(dve.tensor_copy(act_hi[:, :, S:R], ystmp[:]))
            dve.tensor_tensor(act_lo[:, :, S:R], ystmp[:], hi32[:, :, S:R], ALU.subtract).then_inc(sem("s_split"), 2)

            split_weights(KT, NZ)

            dve.wait_ge(sem("h_meaned"), 1)
            for t in range(3):
                dve.tensor_scalar(acc[:, T3 * t:T3 * (t + 1)], psum[:, t, 0:T3], 1.0 / D, EPS, ALU.mult, ALU.add).then_inc(sem("h_eps"), 1)
            for t in range(3):
                dve.wait_ge(sem("h_sqrt"), t + 1)
                dve.reciprocal(acc[:, T3 * t:T3 * (t + 1)], acc[:, T3 * t:T3 * (t + 1)]).then_inc(sem("h_rooted"), 1)
            for i, (r0, n) in enumerate(ROW_TILES):
                dve.wait_ge(sem("p_hi"), i + 1)
                dve.tensor_tensor(pt_lo[:, :, r0:r0 + n], psum[:, 6 + i % 2, 0:2 * n].rearrange("p (m r) -> p m r", m=2),
                                  pt_hi[:, :, r0:r0 + n].bitcast(F32), ALU.subtract).then_inc(sem("p_lo"), 1)
            for k in range(KT):
                dve.wait_ge(sem("h_hi"), k + 1)
                dve.scalar_tensor_tensor(act_lo[:, k, :], h_stage[:, k % 2, :], gcol[:, k:k + 1], hi32[:, k, :], ALU.mult, ALU.subtract).then_inc(sem("h_split"), 1)
            dve.wait_ge(sem("h_rooted"), 3)

            def split_u(n):
                dve.wait_ge(sem("u_loaded"), 32 * (n + 1))
                if n >= 2:
                    dve.wait_ge(sem("u_produced"), 3 * (n - 1))
                dve.tensor_copy(u_hi[:, n % 2], u_raw[:]).then_inc(sem("u_hi_ready"), 1)
                dve.wait_ge(sem("u_hi_ready"), n + 1)
                dve.tensor_tensor(u_lo[:, n % 2], u_raw[:], u_hi[:, n % 2].bitcast(F32), ALU.subtract).then_inc(sem("u_lo_ready"), 1)
            split_u(0)
            for n in range(KT):
                if n + 1 < KT:
                    split_u(n + 1)
                for t in range(3):
                    u = 3 * n + t
                    rows = slice(T3 * t, T3 * (t + 1))
                    dve.wait_ge(sem("u_produced"), u + 1)
                    dve.tensor_tensor(t_gate[:, u % 2, :], psum[:, t, 0:T3], acc[:, rows], ALU.mult).then_inc(sem("g_scaled"), 1)
                    dve.wait_ge(sem("gated"), u + 1)
                    if u >= 2:
                        dve.wait_ge(sem("y_turned"), u - 1)
                    dve.tensor_tensor(t_y[:, u % 2, :], psum[:, 3 + t, 0:T3], t_gate[:, u % 2, :], ALU.mult).then_inc(sem("p_read"), 1)
                    dve.wait_ge(sem("p_read"), u + 1)
                    dve.wait_ge(sem(f"hin_loaded{u % 2}"), 16 * (u // 2 + 1))
                    dve.tensor_tensor(t_y[:, u % 2, :], t_y[:, u % 2, :], h_in[:, u % 2, :], ALU.add).then_inc(sem("h_added"), 1)
            dve.wait_ge(sem("gf_loaded"), 16)
            for i, (r0, n) in enumerate(ROW_TILES):
                dve.wait_ge(sem("f_squared"), i + 1)
                dve.tensor_scalar(small[0:n, 32 + i:33 + i], small[0:n, 32 + i:33 + i], 1.0 / D, EPS, ALU.mult, ALU.add).then_inc(sem("f_meaned"), 1)
                dve.wait_ge(sem("f_rooted"), i + 1)
                chain(dve.reciprocal(small[0:n, 50 + i:51 + i], small[0:n, 41 + i:42 + i]))
                dve.scalar_tensor_tensor(f_out[0:n, i % 2, :], f_in[0:n, i % 3, :], small[0:n, 50 + i:51 + i], gf_row[0:n, :],
                                         ALU.mult, ALU.mult).then_inc(sem("f_scaled"), 1)


_INS = ["x_prompt", "x_sample", "cache_a_k", "cache_a_v", "cache_b_k", "cache_b_v", "p_prompt", "p_sample",
        "g_mix", "w_in", "sinks", "w_out", "g_ple", "w_pg", "w_ple", "g_final"]
_OUTS = [(1, S, D), (NB, 1, D), (1, 1, S, HEADS, HD), (1, 1, S, HEADS, HD), (1, 1, P, KVH, HD), (1, 1, P, KVH, HD),
         (1, NB, 1, HEADS, HD), (1, NB, 1, HEADS, HD), (1, NB, 1, KVH, HD), (1, NB, 1, KVH, HD)]


def kernel(**inputs):
    import concourse.bacc as _bacc
    from concourse.bass_utils import run_bass_kernel_spmd as _run

    nc = _bacc.Bacc("TRN2", target_bir_lowering=False, num_devices=1)
    arrays, aps = {}, {}
    given = {n: np.ascontiguousarray(inputs[n]) for n in _INS}
    given.update(shape_tables())
    for name, x in given.items():
        arrays[f"in_{name}"] = x
        aps[name] = nc.dram_tensor(f"in_{name}", x.shape, F32, kind="ExternalInput").ap()
    outs = [nc.dram_tensor(f"out_{i}", s, F32, kind="ExternalOutput").ap() for i, s in enumerate(_OUTS)]
    build(nc, aps, outs)
    r = _run(nc, [arrays], core_ids=[0])
    return tuple(r.results[0][f"out_{i}"] for i in range(len(_OUTS)))
```

```python
from contextlib import ExitStack

import numpy as np
import concourse.bass as bass
from concourse import mybir

F32 = mybir.dt.float32
F32R = mybir.dt.float32r
ALU = mybir.AluOpType
ACT = mybir.ActivationFunctionType
AX = mybir.AxisListType

P = 128
D = 2048
S = 1024
NB = 8
R = S + NB
KT = D // P
T3 = R // 3
HEADS, HD, KVH = 16, 64, 4
NZ = 52
ZQA, ZKA, ZVA, ZGA, ZQB, ZKB, ZVB, ZGB = 0, 8, 16, 24, 32, 40, 42, 44
PLE = 256
EPS = 1e-6
NEG = -1e30
BLK = P
QB = S // BLK
SCALE = HD ** -0.5
ROW_TILES = [(i * P, P) for i in range(S // P)] + [(S, NB)]
PIECES = [[(0, 128), (128, 128), (256, 88)]] * 3

CHUNKS_A = [(b, k0, min(512, (b + 1) * BLK - k0)) for b in range(QB) for k0 in range(0, (b + 1) * BLK, 512)]
CHUNKS_B = [(b, max(b - 1, 0) * BLK, BLK * min(b + 1, 2)) for b in range(QB)]
PAIRS = HEADS // 2


S_FIRST = 13


def off(kind, b):
    return 0 if kind == "A" else max(b - 1, 0) * BLK


def lag(chunks, b):
    return 3 if last_chunk(chunks, b) == b else 2


def turn_step(chunks):
    return [last_chunk(chunks, b) + lag(chunks, b) + c - min(i for i, x in enumerate(chunks) if x[0] == b)
            for c, (b, _, _) in enumerate(chunks)]


def last_chunk(chunks, b):
    return max(i for i, x in enumerate(chunks) if x[0] == b)


SETS = [(1920, 1, 128), (1536, 4, 96), (0, 16, 96)]
NEAR, MID, FAR = range(3)
SROWS = [128, 97, 96]
SCOL = [0, 128, 225]
NKA, NKB = 321, 129


def shape_tables():
    p = np.arange(P)[:, None]
    u = np.arange(S)[None, :]
    dist = p + (S - BLK) - u
    c = (dist <= 128).astype(int) + ((dist % 4 == 0) & (dist <= 512)) + (dist % 16 == 0)
    logc = np.where((dist >= 0) & (c > 0), np.log(np.maximum(c, 1)), NEG)
    band = np.where((dist >= 0) & (dist <= 128), 0.0, NEG)[:, S - 2 * BLK:]
    slopes = np.exp2(-8.0 * np.arange(1, HEADS + 1) / HEADS).astype(np.float32)
    f = np.float32
    da = np.concatenate([128 - np.arange(128), 512 - 4 * np.arange(96), [0], 2048 - 16 * np.arange(96)])
    ca = (da <= 128).astype(int) + ((da % 4 == 0) & (da <= 512)) + (da % 16 == 0)
    db = np.concatenate([128 - np.arange(128), [0]])
    sa = (-slopes[:, None] * da.astype(f)[None, :]) + np.log(ca).astype(f)[None, :]
    sb = -slopes[:, None] * db.astype(f)[None, :]
    return {
        "c_ident": np.eye(P, dtype=f),
        "c_negd": (-dist).astype(f),
        "c_logc": (logc * 8).astype(f),
        "c_band": (band * 8).astype(f),
        "c_slope": np.broadcast_to(8 * slopes, (P, HEADS)).astype(f).copy(),
        "c_sbias": np.concatenate([8 * sa, 8 * sb], axis=1).astype(f),
    }


def bcast_rows(row, n):
    return bass.AP(tensor=row.tensor, offset=row.offset, ap=[[0, n]] + [list(x) for x in row.ap[1:]])


def build(nc, a, o):
    (y_prompt, y_sample, ak_p, av_p, bk_p, bv_p, ak_s, av_s, bk_s, bv_s) = o
    w_in = a["w_in"][0].rearrange("(k p) n -> p k n", p=P)
    w_out = a["w_out"][0].rearrange("(k p) n -> p k n", p=P)
    w_pg = a["w_pg"][0].rearrange("(k p) n -> p k n", p=P)
    w_ple = a["w_ple"][0].rearrange("(k p) n -> p k n", p=P)
    x_p, x_s = a["x_prompt"][0], a["x_sample"].rearrange("b t d -> (b t) d")
    p_p, p_s = a["p_prompt"][0, 0], a["p_sample"][0].rearrange("b t d -> (b t) d")
    yp, ys = y_prompt[0], y_sample.rearrange("b t d -> (b t) d")

    z_dram = nc.dram_tensor("z_scratch", [NZ, P, R], F32, kind="Internal").ap()
    h_dram = nc.dram_tensor("h_scratch", [KT, P, R], F32, kind="Internal").ap()
    y_dram = nc.dram_tensor("y_scratch", [R, D], F32, kind="Internal").ap()
    q_dram = nc.dram_tensor("q_scratch", [NB, D], F32, kind="Internal").ap()

    ctx = ExitStack()
    sem_list = {}

    def sem(name):
        if name not in sem_list:
            sem_list[name] = ctx.enter_context(nc.semaphore(name))
        return sem_list[name]

    with ctx:
        def keep(name, shape, dt=F32):
            return ctx.enter_context(nc.sbuf_tensor(name, shape, dt))

        act_hi = keep("act_hi", [P, KT, R], F32R)
        act_lo = keep("act_lo", [P, KT, R], F32R)
        ident = keep("ident", [P, P])
        small = keep("small", [P, 64])
        ysm = keep("ysm", [P, KT, NB])
        hi32 = act_hi[:].bitcast(F32)

        psum = ctx.enter_context(nc.psum_tensor("psum", [P, 8, 512], F32))

        def phase(tensors):
            with ExitStack() as st:
                return [st.enter_context(nc.sbuf_tensor(n, s, d)) for n, s, d in tensors]

        x_in, x_n, g_row = phase([("x_in", [P, 2, D], F32), ("x_n", [P, 2, D], F32), ("g_row", [P, D], F32)])
        w_sizes = [("w_lo", [P, 2, KT, P], F32R), ("w_hi", [P, 2, KT, P], F32R), ("w_raw", [P, 2, KT, P], F32)]
        with ExitStack() as own:
            stage = own.enter_context(nc.sbuf_tensor("stage", [P, 2, R], F32))
            _, w_lo, w_hi, w_raw = [own.enter_context(nc.sbuf_tensor(n, sh, d)) for n, sh, d in [("beside_place", [P, 22016 // 4], F32)] + w_sizes]
        with ExitStack() as own:
            own.enter_context(nc.sbuf_tensor("stage_place", [P, 2, R], F32))
            s_ring, s_q, s_prod, s_prob, s_prob_t, s_bias, s_sc, s_row = phase([
                ("s_ring", [P, 3, S], F32), ("s_q", [P, S], F32), ("s_prod", [P, 512], F32), ("s_prob", [HEADS, NKA], F32),
                ("s_prob_t", [P, 3, HEADS], F32), ("s_bias", [HEADS, NKA], F32), ("s_sc", [P, 3, HEADS], F32),
                ("s_row", [HEADS, 8], F32)])
            acc, sq, x_cols, ones = phase([("acc", [P, R], F32), ("sq", [P, R], F32), ("x_cols", [P, 2, 9, P], F32), ("ones", [P, P], F32)])
        with ExitStack() as own:
            h_in, t_gate, t_y = [own.enter_context(nc.sbuf_tensor(n, [P, 2, T3], F32)) for n in ("h_in", "t_gate", "t_y")]
            own.enter_context(nc.sbuf_tensor("acc_place", [P, R], F32))
            u_raw, u_even, u_odd, pt_hi, pt_lo, y_nat, gcol = phase([
                ("u_raw", [P, KT + 2, P], F32), ("u_even", [P, 2, KT + 2, P], F32R), ("u_odd", [P, 2, KT + 2, P], F32R),
                ("pt_hi", [P, 2, R], F32R), ("pt_lo", [P, 2, R], F32R), ("y_nat", [P, 2, 3, P], F32), ("gcol", [P, KT], F32)])
            own.enter_context(nc.sbuf_tensor("u_place", [P, 3, KT + 2, P], F32))
            h_stage, = phase([("h_stage", [P, 4, R], F32)])
        u_hi, u_lo = [u_even[:, 0], u_odd[:, 0]], [u_even[:, 1], u_odd[:, 1]]
        zq, zk, zg, zv, v_nat, k_nat, prob, prob_t, bias, negd, mask, slope, sink, mx, yt = phase([
            ("zq", [P, 2, 2, S], F32), ("zk", [P, 2, S], F32), ("zg", [P, S], F32), ("zv", [P, S], F32),
            ("v_nat", [P, QB, P], F32), ("k_nat", [P, 4, P], F32),
            ("prob", [P, 2 * 1024 + 2 * 896], F32), ("prob_t", [P, 2, 512], F32), ("bias", [P, 2, S], F32),
            ("negd", [P, S], F32), ("mask", [P, S], F32), ("slope", [P, HEADS], F32),
            ("sink", [P, HEADS], F32), ("mx", [P, 4, 24], F32), ("yt", [P, 512], F32)])
        zst, zn, kb, vb, vb_new, q_ring, bprod, bprob, bprob_t, bnew_t, bbias, ssink, bsc, bnew, brow, ystmp = phase([
            ("zst", [P, NZ, NB], F32), ("zn", [NB, 12, P], F32), ("kb", [P, NB, 256], F32), ("vb", [P, NB, 256], F32),
            ("vb_new", [1, NB, 256], F32), ("q_ring", [P, 4, S], F32), ("bprod", [P, S], F32),
            ("bprob", [HEADS, NB, NKB], F32), ("bprob_t", [P, NB, HEADS], F32), ("bnew_t", [1, NB, HEADS], F32),
            ("bbias", [HEADS, NKB], F32), ("ssink", [HEADS, 1], F32), ("bsc", [P, NB, HEADS], F32), ("bnew", [NB, HEADS], F32),
            ("brow", [HEADS, 6, NB], F32), ("ystmp", [P, KT, NB], F32)])

        f_in, f_out, gf_row = phase([("f_in", [P, 3, D], F32), ("f_out", [P, 2, D], F32), ("gf_row", [P, D], F32)])

        zsa = s_q[:, 0:24 * NB].rearrange("p (t n) -> p t n", n=NB)
        PLACE_A, PLACE_BACK = [0, 1, 3, 6, 10, 0, 8, 0], {"A": [2, 3, 4, 4, 5, 3, 2, 2], "B": [4] * QB}

        def prob_of(n, b):
            kind, j = pairs[n]
            w = b + 1 if kind == "A" else min(b + 1, 2)
            place = 2 * (b % 4) if kind == "B" else PLACE_A[b] if j % 2 == 0 else 15 - PLACE_A[b] - w
            return prob[:, 2 * BLK * place:2 * BLK * (place + w)].rearrange("p (h n) -> p h n", h=2)

        def place_wait(eng, n, b):
            kind, j = pairs[n]
            before = QB * n + b - ((2, 3)[b] if kind == "B" and j == 0 and b < 2 else PLACE_BACK[kind][b])
            if before >= 0:
                n2, b2 = divmod(before, QB)
                pair_wait(eng, "turned", n2, 2 * (last_chunk(chunks_of(pairs[n2][0]), b2) + 1))
        pairs = [("A", j) for j in range(PAIRS)] + [("B", j) for j in range(PAIRS)]
        NT = NZ + KT

        def chunks_of(kind):
            return CHUNKS_A if kind == "A" else CHUNKS_B

        def nat_groups(kind):
            if kind == "A":
                return [("v", range(0, 4), 2), ("v", range(4, 8), 4), ("k", range(0, 4), 5), ("k", range(4, 8), 8)]
            return [("v", range(0, 4), 2), ("v", range(4, 8), 4), ("k", range(7, 8), 5)]

        def walk(visit):
            for n, (kind, j) in enumerate(pairs):
                for s in range(len(chunks_of(kind))):
                    visit(n, s)
            kind = pairs[-1][0]
            for s in range(len(chunks_of(kind)), len(chunks_of(kind)) + 5):
                visit(len(pairs) - 1, s)

        def both(n, s):
            if n and s < len(chunks_of(pairs[n][0])):
                yield n - 1, s + len(chunks_of(pairs[n - 1][0]))
            yield n, s

        def per_pair(name, kind):
            return {"scored": 2, "biased": 2, "turned": 2, "copied0": 1, "copied1": 1, "summed": 1}.get(name, 0) * len(chunks_of(kind)) \
                or {"shifted": QB, "exped": 2 * QB, "scaled": 2 * QB, "y_gated": 2, "nat_turned": len(nat_groups(kind)),
                    "nat_copied": len(nat_groups(kind))}[name]

        def pair_wait(eng, name, n, local):
            if n >= 0:
                kind, j = pairs[n]
                eng.wait_ge(sem(kind + name), per_pair(name, kind) * j + local)

        def buffer_wait(eng, name, n, local):
            if local > 0:
                pair_wait(eng, name, n, local)
            elif n > 0:
                pair_wait(eng, name, n - 1, per_pair(name, pairs[n - 1][0]) + local)

        block = ctx.enter_context(nc.Block())

        @block.sync
        def _(sp):
            sp.dma_start(ident[:], a["c_ident"]).then_inc(sem("consts"), 16)
            sp.dma_start(g_row[:], bcast_rows(a["g_mix"][0:1, :], P)).then_inc(sem("consts"), 16)
            for i, (r0, n) in enumerate(ROW_TILES):
                if i >= 2:
                    sp.wait_ge(sem("x_normed"), i - 1)
                src = x_p[r0:r0 + n, :] if i < 8 else x_s
                sp.dma_start(x_in[0:n, i % 2, :], src).then_inc(sem(f"x_loaded{i % 2}"), 16)
            with sp.Fori(0, NZ // 2) as it:
                for par in range(2):
                    sp.wait_ge(sem("lo_ready"), it * 2 + par + 1)
                    sp.dma_start(w_raw[:, par], w_in[:, :, bass.ds(it * (2 * P) + par * P, P)]).then_inc(sem(f"w_loaded{par}"), 16)
            sp.wait_ge(sem("produced"), 3 * (2 + NZ))
            sp.wait_ge(sem("z_stored0"), 16 * (NZ // 2 + 1))
            sp.wait_ge(sem("z_stored1"), 16 * (NZ // 2 + 1))
            near, far = slice(S // 2, S), slice(0, S // 2)
            sp.dma_start(negd[:, near], a["c_negd"][:, near]).then_inc(sem("consts3"), 16)
            sp.dma_start(mask[:, near], a["c_logc"][:, near]).then_inc(sem("consts3"), 16)
            sp.dma_start(slope[:], a["c_slope"]).then_inc(sem("consts3"), 16)
            sp.dma_start(sink[:], bcast_rows(a["sinks"][0:1, :], P)).then_inc(sem("consts3"), 16)
            for n, (kind, j) in enumerate(pairs):
                par = j % 2
                if n >= 2:
                    pk, pj = pairs[n - 2]
                    sp.wait_ge(sem(pk + "y_gated"), 2 * (pj + 1))
                if n >= 1:
                    pk, pj = pairs[n - 1]
                    sp.wait_ge(sem(pk + "nat_turned"), len(nat_groups(pk)) * pj + 2)
                if kind == "A":
                    for h in range(2):
                        sp.dma_start(zq[HD * h:HD * h + HD, par, h, :], z_dram[ZQA + j, HD * h:HD * h + HD, 0:S]).then_inc(sem(f"Az_loaded{par}"), 16)
                    sp.dma_start(zk[:, par], z_dram[ZKA + j, :, 0:S]).then_inc(sem(f"Az_loaded{par}"), 16)
                    sp.dma_start(zv[:], z_dram[ZVA + j, :, 0:S]).then_inc(sem("Av_loaded"), 16)
                    if j == 0:
                        sp.dma_start(negd[:, far], a["c_negd"][:, far]).then_inc(sem("consts"), 16)
                        sp.dma_start(mask[:, far], a["c_logc"][:, far]).then_inc(sem("consts"), 16)
                else:
                    g = j // 2
                    half = slice(HD * (g % 2), HD * (g % 2) + HD)
                    for d in (0, HD):
                        sp.dma_start(zv[d:d + HD, :], z_dram[ZVB + g // 2, half, 0:S]).then_inc(sem("Bv_loaded"), 16)
                    for h in range(2):
                        sp.dma_start(zq[HD * h:HD * h + HD, par, h, :], z_dram[ZQB + j, HD * h:HD * h + HD, 0:S]).then_inc(sem(f"Bz_loaded{par}"), 16)
                    for d in (0, HD):
                        sp.dma_start(zk[d:d + HD, par, :], z_dram[ZKB + g // 2, half, 0:S]).then_inc(sem(f"Bz_loaded{par}"), 16)
                if kind == "B" and j == 0:
                    sp.wait_ge(sem("bias_built"), 2 * PAIRS)
                    sp.dma_start(mask[:, S - 256:S], a["c_band"]).then_inc(sem("consts3"), 16)
                if n >= 1:
                    pk, pj = pairs[n - 1]
                    sp.wait_ge(sem(pk + "y_gated"), 2 * (pj + 1))
                sp.dma_start(zg[:], z_dram[(ZGA if kind == "A" else ZGB) + j, :, 0:S]).then_inc(sem("zg_loaded"), 16)

            sp.wait_ge(sem("Bv_stored"), 16 * 4)
            sp.wait_ge(sem("Bk_stored"), 16 * 4)
            sp.wait_ge(sem("Ak_stored"), 16 * 16)
            sp.wait_ge(sem("Av_stored"), 16 * 8)
            sp.wait_ge(sem("y_split"), 2 * len(pairs))
            sp.dma_start(zst[:], z_dram[:, :, S:R].rearrange("t p n -> p t n")).then_inc(sem("b_consts"), 16)
            sp.dma_start(bbias[:], a["c_sbias"][:, NKA:NKA + NKB]).then_inc(sem("b_consts"), 16)
            sp.dma_start(ssink[:], a["sinks"].rearrange("a h -> h a")).then_inc(sem("b_consts"), 16)
            sp.dma_start(kb[:], a["cache_b_k"][0].rearrange("b r h d -> r b (h d)")).then_inc(sem("kb_loaded"), 16)
            sp.dma_start(vb[:], a["cache_b_v"][0].rearrange("b r h d -> r b (h d)")).then_inc(sem("vb_loaded"), 16)
            sp.wait_ge(sem("b_rows"), 16 * 3)
            for b in range(NB):
                if b >= 4:
                    sp.wait_ge(sem("b_scored"), b - 3)
                sp.dma_start(q_ring[:, b % 4, :], bcast_rows(q_dram[b:b + 1, S:D], P)).then_inc(sem(f"qb_loaded{b}"), 16)
            sp.dma_start(vb_new[:], bv_s.rearrange("l b t h d -> (l t) b (h d)")).then_inc(sem("vb_loaded"), 16)

            with sp.Fori(0, KT // 2) as it:
                for par in range(2):
                    sp.wait_ge(sem("lo_ready"), it * 2 + (NZ + par + 1))
                    sp.dma_start(w_raw[:, par], w_out[:, :, bass.ds(it * (2 * P) + par * P, P)]).then_inc(sem(f"w_loaded{par}"), 16)
                    sp.wait_ge(sem("s_split"), 2)
                    sp.wait_ge(sem("produced"), 3 * (it * 2 + (NZ + 1 + par)))
                    cols = bass.ds(it * (2 * P) + par * P, P)
                    for t in range(2):
                        q0 = T3 * t
                        sp.dma_start(x_cols[:, par, 3 * t:3 * t + 2, :], x_p[q0:q0 + 256, cols].rearrange("(c p) n -> p c n", p=P)).then_inc(sem(f"xc_loaded{par}"), 16)
                        sp.dma_start(x_cols[0:88, par, 3 * t + 2, :], x_p[q0 + 256:q0 + 344, cols]).then_inc(sem(f"xc_loaded{par}"), 16)
                    sp.dma_start(x_cols[:, par, 6:8, :], x_p[688:944, cols].rearrange("(c p) n -> p c n", p=P)).then_inc(sem(f"xc_loaded{par}"), 16)
                    sp.dma_start(x_cols[0:80, par, 8, :], x_p[944:1024, cols]).then_inc(sem(f"xc_loaded{par}"), 16)
                    sp.dma_start(x_cols[80:88, par, 8, :], x_s[:, cols]).then_inc(sem(f"xc_loaded{par}"), 16)

            sp.wait_ge(sem("produced"), 3 * (2 + NT))
            sp.wait_ge(sem("z_stored0"), 16 * (NT // 2 + 1))
            sp.wait_ge(sem("z_stored1"), 16 * (NT // 2 + 1))
            sp.wait_ge(sem("h_summed"), KT)
            sp.dma_start(gcol[:], a["g_ple"].rearrange("a (k p) -> p (a k)", p=P), allow_slow_non_contiguous=True).then_inc(sem("gcol_loaded"), 16)
            def load_u(n):
                if n:
                    sp.wait_ge(sem("u_lo_ready"), n)
                sp.dma_start(u_raw[:, 0:KT, :], w_pg[:, :, n * P:(n + 1) * P]).then_inc(sem("u_loaded"), 16)
                sp.dma_start(u_raw[:, KT:, :], w_ple[:, :, n * P:(n + 1) * P]).then_inc(sem("u_loaded"), 16)

            for k in range(KT):
                if k >= 4:
                    sp.wait_ge(sem("h_split"), k - 3)
                sp.dma_start(h_stage[:, k % 4, :], h_dram[k]).then_inc(sem(f"h_loaded{k % 4}"), 16)
                if k < len(ROW_TILES):
                    r0, n = ROW_TILES[k]
                    if k >= 2:
                        sp.wait_ge(sem("p_turned"), k - 1)
                    src = p_p[r0:r0 + n, :] if k < 8 else p_s
                    sp.dma_start(y_nat[0:n, k % 2, 0:2, :].rearrange("p c n -> p (c n)"), src).then_inc(sem(f"p_loaded{k % 2}"), 16)
                if k == 4:
                    load_u(0)
            for n in range(KT):
                if n + 1 < KT:
                    load_u(n + 1)
                for t in range(3):
                    u = 3 * n + t
                    if u >= 2:
                        sp.wait_ge(sem("h_added"), u - 1)
                    sp.dma_start(h_in[:, u % 2, :], h_dram[n, :, T3 * t:T3 * (t + 1)]).then_inc(sem(f"hin_loaded{u % 2}"), 16)
            sp.wait_ge(sem("u_produced"), 3 * KT)
            for par in range(2):
                sp.wait_ge(sem(f"y_stored{par}"), 16 * 3 * KT)
            sp.dma_start(gf_row[:], bcast_rows(a["g_final"].rearrange("(a d) -> a d", a=1), P)).then_inc(sem("gf_loaded"), 16)
            for i, (r0, n) in enumerate(ROW_TILES):
                if i >= 3:
                    sp.wait_ge(sem("f_scaled"), i - 2)
                sp.dma_start(f_in[0:n, i % 3, :], y_dram[r0:r0 + n, :]).then_inc(sem(f"f_loaded{i % 3}"), 16)
            sp.wait_ge(sem("out_stored0"), 16 * 5)
            sp.wait_ge(sem("out_stored1"), 16 * 4)

        @block.gpsimd
        def _(pool):
            rows = lambda ap: ap.rearrange("l b t h d -> (l b t) (h d)")
            pool.wait_ge(sem("z_stored0"), 16 * 13)
            pool.wait_ge(sem("z_stored1"), 16 * 13)
            pool.dma_start(zsa, z_dram[0:24, :, S:R].rearrange("t p n -> p t n")).then_inc(sem("sa_loaded"), 16)
            pool.dma_start(s_bias[:], a["c_sbias"][:, 0:NKA]).then_inc(sem("sa_loaded"), 16)
            pool.wait_ge(sem("sa_copied"), 6)
            sr = s_ring[0:NB].rearrange("p c n -> p (c n)")
            pool.dma_start(q_dram[:, 0:S], sr[:, 0:S]).then_inc(sem("sa_rows"), 16)
            pool.dma_start(rows(ak_s), sr[:, S:2 * S]).then_inc(sem("sa_rows"), 16)
            pool.dma_start(rows(av_s), sr[:, 2 * S:3 * S]).then_inc(sem("sa_rows"), 16)
            pool.wait_ge(sem("sa_rows"), 48)
            with pool.Fori(0, NB) as b:
                pool.wait_ge(sem("sa_scored"), b + 1)
                pool.sem_inc(sem("sample_turn"), 1)
                pool.dma_start(s_q[:], bcast_rows(q_dram[bass.ds(b, 1), 0:S], P)).then_inc(sem("sq_loaded"), 16)
                for i, (cache, new, (r0, step, n)) in enumerate([(a["cache_a_k"], ak_s, x) for x in SETS] + [(a["cache_a_v"], av_s, x) for x in SETS]):
                    t = i % 3
                    if i < 3:
                        pool.wait_ge(sem("sv_used"), b * 3 + i + 1)
                    else:
                        pool.wait_ge(sem("sk_used"), b * 3 + t + 1)
                    pool.sem_inc(sem("sample_turn"), 1)
                    pool.dma_start(s_ring[0:n, t, :], cache[0, bass.ds(b, 1), r0:r0 + step * (n - 1) + 1:step].rearrange("b r h d -> (b r) (h d)")
                                   ).then_inc(sem(f"s{'kv'[i // 3]}_loaded{t}"), 16)
                    if t == MID:
                        pool.dma_start(s_ring[96:97, MID, :], new[0, bass.ds(b, 1)].rearrange("b t h d -> (b t) (h d)")
                                       ).then_inc(sem(f"s{'kv'[i // 3]}_loaded{t}"), 16)
            def visit(n_, s_):
                for n, s in both(n_, s_):
                    kind, j = pairs[n]
                    ch, turn = chunks_of(kind), turn_step(chunks_of(kind))
                    groups = nat_groups(kind)
                    for gi, (what, blks, at) in enumerate(groups):
                        if at != s or (what == "v" and gi == 0):
                            continue
                        if kind == "A":
                            pool.wait_ge(sem("Anat_copied"), 4 * j + gi + 1)
                            if what == "v":
                                pool.dma_start(av_p[0, 0, :, 2 * j:2 * j + 2, :].rearrange("(c p) h d -> p c (h d)", p=P),
                                               v_nat[:]).then_inc(sem("Av_stored"), 16)
                            else:
                                pool.dma_start(ak_p[0, 0, blks[0] * P:(blks[-1] + 1) * P, 2 * j:2 * j + 2, :].rearrange("(c p) h d -> p c (h d)", p=P),
                                               k_nat[:]).then_inc(sem("Ak_stored"), 16)
                        elif j % 2 == 0:
                            pool.wait_ge(sem("Bnat_copied"), 3 * j + gi + 1)
                            if what == "v":
                                pool.dma_start(bv_p[0, 0, :, j // 2, :], v_nat[:, 7, 0:HD]).then_inc(sem("Bv_stored"), 16)
                            else:
                                pool.dma_start(bk_p[0, 0, :, j // 2, :], k_nat[:, 0, 0:HD]).then_inc(sem("Bk_stored"), 16)
                    for half in range(2):
                        if turn[last_chunk(ch, 4 * half + 3)] + 1 == s:
                            pool.wait_ge(sem(kind + "y_gated"), 2 * j + half + 1)
                            dst = slice(512 * half, 512 * half + 512)
                            pool.tensor_copy(act_hi[:, n, dst], yt[:]).then_inc(sem("y_hi"), 1)
                            pool.wait_ge(sem("y_hi"), 2 * n + half + 1)
                            pool.tensor_tensor(act_lo[:, n, dst], yt[:], hi32[:, n, dst], ALU.subtract).then_inc(sem("y_split"), 1)
            walk(visit)

            pool.wait_ge(sem("b_copied"), 3)
            zr = zn[:].rearrange("p c n -> p (c n)")
            pool.dma_start(q_dram[:, S:D], zr[:, 0:S]).then_inc(sem("b_rows"), 16)
            pool.dma_start(rows(bk_s), zr[:, S:S + 256]).then_inc(sem("b_rows"), 16)
            pool.dma_start(rows(bv_s), zr[:, S + 256:S + 512]).then_inc(sem("b_rows"), 16)

            pool.wait_ge(sem("s_split"), 2)
            pool.memset(ones[:], 1.0).then_inc(sem("ones_set"), 1)
            pool.memset(acc[:], 0.0).then_inc(sem("acc_set"), 1)
            pool.sem_inc(sem("h_squared"), 2)
            pool.wait_ge(sem("acc_set"), 1)
            with pool.Fori(0, KT // 2) as it:
                for par in range(2):
                    pool.wait_ge(sem("bank_free"), it * 6 + (6 + 3 * NZ + 3 * par + 3))
                    pool.tensor_tensor(sq[:], stage[:, par], stage[:, par], ALU.mult).then_inc(sem("h_squared"), 1)
                    pool.wait_ge(sem("h_squared"), it * 2 + (par + 3))
                    pool.tensor_tensor(acc[:], acc[:], sq[:], ALU.add).then_inc(sem("h_summed"), 1)
                    pool.wait_ge(sem("h_summed"), it * 2 + par + 1)

            for n in range(KT):
                for t in range(3):
                    u = 3 * n + t
                    pool.wait_ge(sem("y_copied"), u + 1)
                    q0 = T3 * t
                    pool.dma_start(y_dram[q0:q0 + 256, n * P:(n + 1) * P].rearrange("(c p) n -> p c n", p=P), y_nat[:, u % 2, 0:2, :]).then_inc(sem(f"y_stored{u % 2}"), 16)
                    pool.dma_start(y_dram[q0 + 256:q0 + T3, n * P:(n + 1) * P], y_nat[0:88, u % 2, 2, :]).then_inc(sem(f"y_stored{u % 2}"), 16)
            for i, (r0, n) in enumerate(ROW_TILES):
                pool.wait_ge(sem("f_scaled"), i + 1)
                dst = yp[r0:r0 + n, :] if i < 8 else ys
                pool.dma_start(dst, f_out[0:n, i % 2, :]).then_inc(sem(f"out_stored{i % 2}"), 16)

        @block.tensor
        def _(pe):
            pe.wait_ge(sem("consts"), 32)
            for i, (r0, n) in enumerate(ROW_TILES):
                pe.wait_ge(sem("x_normed"), i + 1)
                for q in range(4):
                    u = 4 * i + q
                    if u >= 8:
                        pe.wait_ge(sem("x_lo"), u - 7)
                    for m in range(4):
                        k = 4 * q + m
                        mm = pe.transpose(psum[:, u % 8, n * m:n * m + n], x_n[0:n, i % 2, k * P:(k + 1) * P], ident[0:n, 0:n])
                    mm.then_inc(sem("x_turned"), 1)

            def product(bank, par, hi_w, lo_w, hi_a, lo_a, t, tiles, close, between=None):
                rows = slice(T3 * t, T3 * (t + 1))
                for k in range(tiles):
                    pe.matmul(psum[:, bank, 0:T3], hi_w(k), hi_a[:, k, rows], start=(k == 0), stop=False, skip_group_check=True)
                    pe.matmul(psum[:, bank, 0:T3], hi_w(k), lo_a[:, k, rows], start=False, stop=False, skip_group_check=True)
                    mm = pe.matmul(psum[:, bank, 0:T3], lo_w(k), hi_a[:, k, rows], start=False,
                                   stop=(close and k == tiles - 1), skip_group_check=True)
                    if between and k < tiles - 1:
                        between(k)
                return mm

            pe.sem_inc(sem("produced"), 6)
            pe.wait_ge(sem("x_lo"), 4 * len(ROW_TILES))
            def tiles(first, last, beside):
                with pe.Fori(first, last) as it:
                    for par in range(2):
                        pe.wait_ge(sem("lo_ready"), it * 2 + (par + 3))
                        for t in range(3):
                            pe.wait_ge(sem("bank_free"), it * 6 + (3 * par + t + 1))
                            product(3 * par + t, par, lambda k: w_hi[:, par, k, :], lambda k: w_lo[:, par, k, :],
                                    act_hi, act_lo, t, KT, True, lambda k: beside(it, 3 * par + t, k)).then_inc(sem("produced"), 1)

            def sample_a(it, unit, k):
                count = it - (S_FIRST - 1)
                if unit == 1 and k < 3:
                    t = k
                    if t == 0:
                        pe.wait_ge(sem("sa_scored"), count + 1)
                    mm = pe.transpose(psum[0:HEADS, 6, SCOL[t]:SCOL[t] + SROWS[t]], s_sc[0:SROWS[t], t, :], ident[0:SROWS[t], 0:SROWS[t]])
                    if t == 2:
                        mm.then_inc(sem("sa_rowed"), 1)
                if unit == 3 and k < 3:
                    t = k
                    if t == 0:
                        pe.wait_ge(sem("sa_scaled"), count)
                        pe.sem_inc(sem("sample_turn_pe"), 1)
                    mm = pe.transpose(psum[0:SROWS[t], 7, 16 * t:16 * t + 16], s_prob[:, SCOL[t]:SCOL[t] + SROWS[t]], ident[0:HEADS, 0:HEADS])
                    if t == 2:
                        mm.then_inc(sem("sa_pturned"), 1)
                if unit == 4 and k < 12:
                    t = k // 4
                    if k == 0:
                        pe.wait_ge(sem("sa_pcopied"), count * 3)
                    if k % 4 == 0:
                        pe.wait_ge(sem(f"sv_loaded{t}"), count * (32 if t == MID else 16))
                    for j in (2 * (k % 4), 2 * (k % 4) + 1):
                        mm = pe.matmul(psum[:, 7, 64 + 2 * j:66 + 2 * j], s_ring[0:SROWS[t], t, P * j:P * (j + 1)],
                                       s_prob_t[0:SROWS[t], t, 2 * j:2 * j + 2], start=(k == 0 and j == 0), stop=(t == 2), skip_group_check=True)
                    if k % 4 == 3:
                        mm.then_inc(sem("sv_used"), 1)

            pe.sem_inc(sem("sv_used"), 3)
            tiles(0, S_FIRST, lambda it, u, k: None)
            pe.wait_ge(sem("sa_loaded"), 32)
            for g in range(6):
                if g >= 2:
                    pe.wait_ge(sem("sa_copied"), g - 1)
                for m in range(4):
                    mm = pe.transpose(psum[0:NB, 6 + g % 2, m * P:(m + 1) * P], zsa[:, 4 * g + m, :], ident[:])
                mm.then_inc(sem("sa_turned"), 1)
            tiles(S_FIRST, S_FIRST + NB, sample_a)
            tiles(S_FIRST + NB, NZ // 2, lambda it, u, k: None)

            def visit(n_, s_):
                kind, j = pairs[n_]
                ch = chunks_of(kind)
                c = s_
                if c == 0:
                    if n_ == 0:
                        pe.wait_ge(sem("q_zeroed"), 4)
                    pe.wait_ge(sem(f"{kind}z_loaded{j % 2}"), 16 * (3 if kind == "A" else 4) * (j // 2 + 1))
                if c < len(ch):
                    b, k0, nk = ch[c]
                    for h in range(2):
                        buffer_wait(pe, "biased", n_, 2 * (c - 2) + h + 1)
                        pe.matmul(psum[:, 2 * h + c % 2, 0:nk], zq[:, j % 2, h, b * BLK:(b + 1) * BLK],
                                  zk[:, j % 2, k0:k0 + nk], start=True, stop=True).then_inc(sem(kind + "scored"), 1)
                for n, s in both(n_, s_):
                    kind, j = pairs[n]
                    ch = chunks_of(kind)
                    turn = turn_step(ch)
                    for c, (b, k0, nk) in enumerate(ch):
                        if turn[c] == s:
                            for h in range(2):
                                pair_wait(pe, "scaled", n, 2 * b + h + 1)
                                buffer_wait(pe, f"copied{h}", n, c)
                                for x in range(nk // P):
                                    mm = pe.transpose(psum[:, 4 + h, x * P:(x + 1) * P], prob_of(n, b)[:, h, k0 - off(kind, b) + x * P:k0 - off(kind, b) + (x + 1) * P], ident[:])
                                mm.then_inc(sem(kind + "turned"), 1)
                    for c, (b, k0, nk) in enumerate(ch):
                        if turn[c] + 1 == s:
                            if b % 4 == 0 and c == last_chunk(ch, b - 1) + 1 if b else c == 0:
                                buffer_wait(pe, "y_gated", n, b // 4)
                            if c == 0:
                                pair_wait(pe, "nat_copied", n, 1)
                            if b == 4:
                                pair_wait(pe, "nat_copied", n, 2)
                            first = k0 == off(kind, b)
                            last = k0 + nk == (b + 1) * BLK
                            for h in range(2):
                                pair_wait(pe, f"copied{h}", n, c + 1)
                                for x in range(nk // P):
                                    mm = pe.matmul(psum[HD * h:HD * h + HD, 6, (b % 4) * P:(b % 4 + 1) * P],
                                                   v_nat[:, k0 // P + x, HD * h:HD * h + HD], prob_t[:, h, x * P:(x + 1) * P],
                                                   start=(b % 4 == 0 and first and x == 0), stop=(last and x == nk // P - 1), skip_group_check=True)
                            mm.then_inc(sem(kind + "summed"), 1)
                kind, j = pairs[n_]
                for gi, (what, blks, at) in enumerate(nat_groups(kind)):
                    if at == s_:
                        if gi == 0:
                            pe.wait_ge(sem(kind + "v_loaded"), 16 * (1 if kind == "A" else 2) * (j + 1))
                        buffer_wait(pe, "nat_copied", n_, gi)
                        for x, blk in enumerate(blks):
                            src = zv[:, blk * P:(blk + 1) * P] if what == "v" else zk[:, j % 2, blk * P:(blk + 1) * P]
                            mm = pe.transpose(psum[:, 7, x * P:(x + 1) * P], src, ident[:])
                        mm.then_inc(sem(kind + "nat_turned"), 1)
            walk(visit)

            pe.wait_ge(sem("b_consts"), 48)
            for g in range(3):
                for m in range(4):
                    mm = pe.transpose(psum[0:NB, g, m * P:(m + 1) * P], zst[:, ZQB + 4 * g + m, :], ident[:])
                mm.then_inc(sem("b_turned"), 1)
            pe.wait_ge(sem("bnew_scored"), 1)
            pe.transpose(psum[0:HEADS, 3, 0:NB], bnew[:], ident[0:NB, 0:NB]).then_inc(sem("bnew_rowed"), 1)
            pe.wait_ge(sem("b_copied"), 3)
            for b in range(NB):
                pe.wait_ge(sem("b_scored"), b + 1)
                mm = pe.transpose(psum[0:HEADS, b // 4, P * (b % 4):P * (b % 4 + 1)], bsc[:, b, :], ident[:])
                mm.then_inc(sem("b_rowed"), 1)
            pe.wait_ge(sem("b_scaled"), 1)
            for b in range(NB):
                pe.transpose(psum[:, 4, 16 * b:16 * b + 16], bprob[:, b, 0:P], ident[0:HEADS, 0:HEADS])
                mm = pe.transpose(psum[0:1, 5, 16 * b:16 * b + 16], bprob[:, b, P:NKB], ident[0:HEADS, 0:HEADS])
            mm.then_inc(sem("b_pturned"), 1)
            pe.wait_ge(sem("b_pcopied"), 2)
            pe.wait_ge(sem("vb_loaded"), 32)
            for b in range(NB):
                for g in range(KVH):
                    c0 = 16 * b + 4 * g
                    pe.matmul(psum[0:HD, 6, c0:c0 + 4], vb[:, b, HD * g:HD * (g + 1)], bprob_t[:, b, 4 * g:4 * g + 4], start=True, stop=False)
                    mm = pe.matmul(psum[0:HD, 6, c0:c0 + 4], vb_new[:, b, HD * g:HD * (g + 1)], bnew_t[:, b, 4 * g:4 * g + 4], start=False, stop=True)
            mm.then_inc(sem("b_summed"), 1)

            pe.wait_ge(sem("s_split"), 2)
            with pe.Fori(0, KT // 2) as it:
                for par in range(2):
                    pe.wait_ge(sem("lo_ready"), it * 2 + (NZ + par + 3))
                    for t in range(3):
                        bank = 3 * par + t
                        pe.wait_ge(sem("bank_free"), it * 6 + (3 * NZ + 3 * par + t + 1))
                        product(bank, par, lambda k: w_hi[:, par, k, :], lambda k: w_lo[:, par, k, :], act_hi, act_lo, t, KT, False)
                        if t == 0:
                            pe.wait_ge(sem(f"xc_loaded{par}"), it * 112 + 112)
                        for x, (c0, n) in enumerate(PIECES[t]):
                            mm = pe.matmul(psum[:, bank, c0:c0 + n], x_cols[0:n, par, 3 * t + x, :], ident[0:n, 0:n], start=False, stop=(x == 2), skip_group_check=True)
                        mm.then_inc(sem("produced"), 1)

            pe.wait_ge(sem("h_summed"), KT)
            pe.wait_ge(sem("bank_free"), 3 * NT + 6)
            for t in range(3):
                mm = pe.matmul(psum[:, t, 0:T3], ones[:], acc[:, T3 * t:T3 * (t + 1)], start=True, stop=True)
            mm.then_inc(sem("h_meaned"), 1)
            for i, (r0, n) in enumerate(ROW_TILES):
                pe.wait_ge(sem(f"p_loaded{i % 2}"), 16 * (i // 2 + 1))
                if i >= 2:
                    pe.wait_ge(sem("p_lo"), i - 1)
                for m in range(2):
                    mm = pe.transpose(psum[:, 6 + i % 2, n * m:n * m + n], y_nat[0:n, i % 2, m, :], ident[0:n, 0:n])
                mm.then_inc(sem("p_turned"), 1)
            pe.wait_ge(sem("p_lo"), len(ROW_TILES))
            pe.wait_ge(sem("h_rooted"), 3)
            pe.wait_ge(sem("h_split"), 1)

            def y_turn(u):
                pe.wait_ge(sem("h_added"), u + 1)
                if u >= 2:
                    pe.wait_ge(sem("y_copied"), u - 1)
                for x, (c0, n) in enumerate(PIECES[u % 3]):
                    mm = pe.transpose(psum[0:n, 6 + u % 2, x * P:(x + 1) * P], t_y[:, u % 2, c0:c0 + n], ident[:])
                mm.then_inc(sem("y_turned"), 1)

            for n in range(KT):
                par = n % 2
                pe.wait_ge(sem("u_lo_ready"), n + 1)
                for t in range(3):
                    u = 3 * n + t
                    if u >= 3:
                        pe.wait_ge(sem("p_read"), u - 2)
                    follow = (lambda k: pe.wait_ge(sem("h_split"), k + 2)) if u == 0 else None
                    product(t, par, lambda k: u_hi[par][:, k, :], lambda k: u_lo[par][:, k, :], act_hi, act_lo, t, KT, True, follow)
                    mm = product(3 + t, par, lambda k: u_hi[par][:, KT + k, :], lambda k: u_lo[par][:, KT + k, :], pt_hi, pt_lo, t, 2, True)
                    mm.then_inc(sem("u_produced"), 1)
                    if u >= 1:
                        y_turn(u - 1)
            y_turn(3 * KT - 1)

        @block.scalar
        def _(act):
            def x_hi_copies(i):
                r0, n = ROW_TILES[i]
                for q in range(4):
                    u = 4 * i + q
                    act.wait_ge(sem("x_turned"), u + 1)
                    act.activation(act_hi[:, 4 * q:4 * q + 4, r0:r0 + n], psum[:, u % 8, 0:4 * n].rearrange("p (m r) -> p m r", m=4), ACT.Copy).then_inc(sem("x_hi"), 1)
            for i, (r0, n) in enumerate(ROW_TILES):
                act.wait_ge(sem(f"x_loaded{i % 2}"), 16 * (i // 2 + 1))
                if i >= 2:
                    act.wait_ge(sem("x_turned"), 4 * (i - 1))
                act.activation(x_n[0:n, i % 2, :], x_in[0:n, i % 2, :], ACT.Square, accum_out=small[0:n, i:i + 1]).then_inc(sem("x_squared"), 1)
                act.wait_ge(sem("x_meaned"), i + 1)
                act.activation(small[0:n, 9 + i:10 + i], small[0:n, i:i + 1], ACT.Sqrt).then_inc(sem("x_rooted"), 1)
                if i >= 1:
                    x_hi_copies(i - 1)
            x_hi_copies(8)
            act.wait_ge(sem("x_hi"), 36)
            act.wait_ge(sem("x_lo"), 36)
            act.sem_inc(sem("bank_free"), 6)
            act.sem_inc(sem("z_stored0"), 16)
            act.sem_inc(sem("z_stored1"), 16)
            def stage_tiles(first, last, func, samples):
                with act.Fori(first, last) as it:
                    for par in range(2):
                        act.wait_ge(sem(f"z_stored{par}"), it * 16 + 16)
                        for t in range(3):
                            act.wait_ge(sem("produced"), it * 6 + (3 * par + t + 7))
                            act.activation(stage[:, par, T3 * t:T3 * (t + 1)], psum[:, 3 * par + t, 0:T3], func).then_inc(sem("bank_free"), 1)
                        act.wait_ge(sem("bank_free"), it * 6 + (3 * par + 9))
                        act.dma_start(z_dram[it * 2 + par], stage[:, par]).then_inc(sem(f"z_stored{par}"), 16)
                        if samples and par == 0:
                            act.wait_ge(sem("sa_shifted"), it - (S_FIRST - 1))
                            act.activation(s_prob[:], s_prob[:], ACT.Exp, bias=s_row[:, 1:2], accum_out=s_row[:, 2:3]).then_inc(sem("sa_exped"), 1)

            stage_tiles(0, ZGA // 2, ACT.Copy, False)
            stage_tiles(ZGA // 2, S_FIRST, ACT.Silu, False)
            for g in range(6):
                act.wait_ge(sem("sa_turned"), g + 1)
                act.activation(s_ring[0:NB].rearrange("p c n -> p (c n)")[:, 512 * g:512 * g + 512], psum[0:NB, 6 + g % 2, :], ACT.Copy).then_inc(sem("sa_copied"), 1)
            stage_tiles(S_FIRST, ZQB // 2, ACT.Silu, True)
            stage_tiles(ZQB // 2, S_FIRST + NB, ACT.Copy, True)
            stage_tiles(S_FIRST + NB, ZGB // 2, ACT.Copy, False)
            stage_tiles(ZGB // 2, NZ // 2, ACT.Silu, False)

            def visit(n_, s_):
                for n, s in both(n_, s_):
                    kind, j = pairs[n]
                    ch, turn = chunks_of(kind), turn_step(chunks_of(kind))
                    for c, (b, k0, nk) in enumerate(ch):
                        if turn[c] == s:
                            pair_wait(act, "turned", n, 2 * c + 1)
                            buffer_wait(act, "summed", n, c)
                            act.activation(prob_t[:, 0, 0:nk], psum[:, 4, 0:nk], ACT.Copy).then_inc(sem(kind + "copied0"), 1)
                    if s < len(ch) and s == last_chunk(ch, ch[s][0]):
                        b = ch[s][0]
                        w = (b + 1) * BLK - off(kind, b)
                        pair_wait(act, "shifted", n, b + 1)
                        m = mx[:, b % 4]
                        if kind == "B":
                            for h in range(2):
                                act.activation(m[:, 10 + h:11 + h], sink[:, 2 * j + h:2 * j + h + 1], ACT.Exp, bias=m[:, 4 + h:5 + h])
                        for h in range(2):
                            pr = prob_of(n, b)[:, h, 0:w]
                            act.activation(pr, pr, ACT.Exp, bias=m[:, 4 + h:5 + h], accum_out=m[:, 6 + h:7 + h]).then_inc(sem(kind + "exped"), 1)
                    for gi, (what, blks, at) in enumerate(nat_groups(kind)):
                        if at + (gi == 0) == s:
                            pair_wait(act, "nat_turned", n, gi + 1)
                            w = len(blks) * P
                            if what == "v":
                                if n >= 1 and gi == 0:
                                    pk, pj = pairs[n - 1]
                                    pair_wait(act, "summed", n - 1, len(chunks_of(pk)))
                                    act.wait_ge(sem(pk + "v_stored"), 16 * (pj + 1 if pk == "A" else pj // 2 + 1))
                                dst = v_nat[:, blks[0]:blks[-1] + 1, :].rearrange("p c m -> p (c m)")
                            else:
                                count = (2 * j + gi - 2 if kind == "A" else (j + 1) // 2)
                                if kind == "B":
                                    act.wait_ge(sem("Ak_stored"), 16 * 16)
                                if count:
                                    act.wait_ge(sem(kind + "k_stored"), 16 * count)
                                dst = k_nat[:, 0:len(blks), :].rearrange("p c m -> p (c m)")
                            act.activation(dst, psum[:, 7, 0:w], ACT.Copy).then_inc(sem(kind + "nat_copied"), 1)
            act.wait_ge(sem("consts3"), 64)
            walk(visit)

            for g in range(3):
                act.wait_ge(sem("b_turned"), g + 1)
                act.activation(zn[:, 4 * g:4 * g + 4, :].rearrange("p c m -> p (c m)"), psum[0:NB, g, :], ACT.Copy).then_inc(sem("b_copied"), 1)
            act.wait_ge(sem("b_shifted"), 3)
            act.activation(bprob[:], bprob[:], ACT.Exp).then_inc(sem("b_exped"), 1)
            act.activation(brow[:, 2, :], brow[:, 2, :], ACT.Exp).then_inc(sem("b_exped"), 1)

            with act.Fori(0, KT // 2) as it:
                for par in range(2):
                    act.wait_ge(sem(f"z_stored{par}"), it * 16 + 16 * (NZ // 2 + 1))
                    act.wait_ge(sem("h_squared"), it * 2 + (par + 1))
                    for t in range(3):
                        act.wait_ge(sem("produced"), it * 6 + (3 * NZ + 3 * par + t + 7))
                        act.activation(stage[:, par, T3 * t:T3 * (t + 1)], psum[:, 3 * par + t, 0:T3], ACT.Copy).then_inc(sem("bank_free"), 1)
                    act.wait_ge(sem("bank_free"), it * 6 + (3 * NZ + 3 * par + 9))
                    act.dma_start(h_dram[it * 2 + par], stage[:, par]).then_inc(sem(f"z_stored{par}"), 16)

            for t in range(3):
                act.wait_ge(sem("h_eps"), t + 1)
                act.activation(acc[:, T3 * t:T3 * (t + 1)], acc[:, T3 * t:T3 * (t + 1)], ACT.Sqrt).then_inc(sem("h_sqrt"), 1)
            act.wait_ge(sem("gcol_loaded"), 16)
            for k in range(KT):
                act.wait_ge(sem(f"h_loaded{k % 4}"), 16 * (k // 4 + 1))
                act.activation(act_hi[:, k, :], h_stage[:, k % 4, :], ACT.Copy, scale=gcol[:, k:k + 1]).then_inc(sem("h_hi"), 1)
                if k < len(ROW_TILES):
                    r0, n = ROW_TILES[k]
                    act.wait_ge(sem("p_turned"), k + 1)
                    act.activation(pt_hi[:, :, r0:r0 + n], psum[:, 6 + k % 2, 0:2 * n].rearrange("p (m r) -> p m r", m=2), ACT.Copy).then_inc(sem("p_hi"), 1)

            def y_copy(u):
                act.wait_ge(sem("y_turned"), u + 1)
                if u >= 2:
                    act.wait_ge(sem(f"y_stored{u % 2}"), 32 * (u // 2))
                act.activation(y_nat[:, u % 2, 0:2, :], psum[:, 6 + u % 2, 0:256].rearrange("p (c n) -> p c n", c=2), ACT.Copy)
                act.activation(y_nat[0:88, u % 2, 2, :], psum[0:88, 6 + u % 2, 256:384], ACT.Copy).then_inc(sem("y_copied"), 1)
            for u in range(3 * KT):
                act.wait_ge(sem("g_scaled"), u + 1)
                act.activation(t_gate[:, u % 2, :], t_gate[:, u % 2, :], ACT.Sigmoid).then_inc(sem("gated"), 1)
                if u >= 2:
                    y_copy(u - 2)
            y_copy(3 * KT - 2)
            y_copy(3 * KT - 1)

            for i, (r0, n) in enumerate(ROW_TILES):
                act.wait_ge(sem(f"f_loaded{i % 3}"), 16 * (i // 3 + 1))
                if i >= 2:
                    act.wait_ge(sem(f"out_stored{i % 2}"), 16 * (i // 2))
                act.activation(f_out[0:n, i % 2, :], f_in[0:n, i % 3, :], ACT.Square, accum_out=small[0:n, 32 + i:33 + i]).then_inc(sem("f_squared"), 1)
                act.wait_ge(sem("f_meaned"), i + 1)
                act.activation(small[0:n, 41 + i:42 + i], small[0:n, 32 + i:33 + i], ACT.Sqrt).then_inc(sem("f_rooted"), 1)

        @block.vector
        def _(dve):
            done = [0]

            def chain(ins):
                done[0] += 1
                ins.then_inc(sem("dve_chain"), 1)
                dve.wait_ge(sem("dve_chain"), done[0])

            dve.sem_inc(sem("lo_ready"), 2)
            def inverse_root(n, square, root, out):
                chain(dve.reciprocal(out, root))
                chain(dve.scalar_tensor_tensor(root, out, square, root, ALU.mult, ALU.add))
                chain(dve.tensor_scalar(root, root, 0.5, None, ALU.mult))
                chain(dve.reciprocal(out, root))

            def x_lo_parts(i):
                r0, n = ROW_TILES[i]
                for q in range(4):
                    u = 4 * i + q
                    dve.wait_ge(sem("x_hi"), u + 1)
                    dve.tensor_tensor(act_lo[:, 4 * q:4 * q + 4, r0:r0 + n], psum[:, u % 8, 0:4 * n].rearrange("p (m r) -> p m r", m=4),
                                      hi32[:, 4 * q:4 * q + 4, r0:r0 + n], ALU.subtract).then_inc(sem("x_lo"), 1)
            dve.wait_ge(sem("consts"), 32)
            for i, (r0, n) in enumerate(ROW_TILES):
                dve.wait_ge(sem("x_squared"), i + 1)
                dve.tensor_scalar(small[0:n, i:i + 1], small[0:n, i:i + 1], 1.0 / D, EPS, ALU.mult, ALU.add).then_inc(sem("x_meaned"), 1)
                dve.wait_ge(sem("x_rooted"), i + 1)
                inverse_root(n, small[0:n, i:i + 1], small[0:n, 9 + i:10 + i], small[0:n, 18 + i:19 + i])
                dve.scalar_tensor_tensor(x_n[0:n, i % 2, :], x_in[0:n, i % 2, :], small[0:n, 18 + i:19 + i], g_row[0:n, :],
                                         ALU.mult, ALU.mult).then_inc(sem("x_normed"), 1)
                if i >= 1:
                    x_lo_parts(i - 1)
            x_lo_parts(8)

            def split_weights(first, last, middle, end):
                with dve.Fori(first, last) as it:
                    for par in range(2):
                        dve.wait_ge(sem(f"w_loaded{par}"), it * 16 + 16)
                        dve.wait_ge(sem("produced"), it * 6 + (3 * par + 3))
                        dve.tensor_copy(w_hi[:, par], w_raw[:, par]).then_inc(sem("hi_ready"), 1)
                        dve.wait_ge(sem("hi_ready"), it * 2 + (par + 1))
                        dve.tensor_tensor(w_lo[:, par], w_raw[:, par], w_hi[:, par].bitcast(F32), ALU.subtract).then_inc(sem("lo_ready"), 1)
                        (middle, end)[par](it)

            def sample_scores(it):
                count = it - (S_FIRST - 1)
                dve.wait_ge(sem("sq_loaded"), count * 16)
                for t in range(3):
                    n = SROWS[t]
                    dve.wait_ge(sem(f"sk_loaded{t}"), count * (32 if t == MID else 16))
                    for half in range(2):
                        cols = slice(512 * half, 512 * half + 512)
                        m = dve.tensor_tensor(s_prod[0:n, :], s_ring[0:n, t, cols], s_q[0:n, cols], ALU.mult)
                        m.then_inc(sem("s_prods" if half == 0 else "sk_used"), 1)
                        if half == 0:
                            dve.wait_ge(sem("s_prods"), count * 3 + (t - 2))
                        else:
                            dve.wait_ge(sem("sk_used"), count * 3 + (t - 2))
                        m = dve.tensor_reduce(s_sc[0:n, t, 8 * half:8 * half + 8], s_prod[0:n, :].rearrange("p (h d) -> p h d", d=HD), AX.X, ALU.add)
                        last = t == 2 and half == 1
                        m.then_inc(sem("sa_scored" if last else "s_summed"), 1)
                        if not last:
                            dve.wait_ge(sem("s_summed"), count * 5 + (2 * t + half - 4))

            def sample_softmax(it):
                count = it - (S_FIRST - 1)
                dve.wait_ge(sem("sa_loaded"), 32)
                dve.wait_ge(sem("sa_rowed"), count)
                dve.tensor_tensor_reduce(s_prob[:], psum[0:HEADS, 6, 0:NKA], s_bias[:], SCALE, -3e38, ALU.add, ALU.max, s_row[:, 0:1]).then_inc(sem("sa_biased"), 1)
                dve.wait_ge(sem("sa_biased"), count)
                dve.tensor_scalar(s_row[:, 1:2], s_row[:, 0:1], -1.0, None, ALU.mult).then_inc(sem("sa_shifted"), 1)
                dve.wait_ge(sem("sa_exped"), count)
                dve.reciprocal(s_row[:, 3:4], s_row[:, 2:3]).then_inc(sem("sa_inverted"), 1)
                dve.wait_ge(sem("sa_inverted"), count)
                dve.tensor_scalar(s_prob[:], s_prob[:], s_row[:, 3:4], None, ALU.mult).then_inc(sem("sa_scaled"), 1)
                dve.wait_ge(sem("sa_pturned"), count)
                for t in range(3):
                    dve.tensor_copy(s_prob_t[0:SROWS[t], t, :], psum[0:SROWS[t], 7, 16 * t:16 * t + 16]).then_inc(sem("sa_pcopied"), 1)
                dve.wait_ge(sem("sv_used"), count * 3 + 3)
                for h in range(2):
                    half = slice(HD * h, HD * h + HD)
                    dve.tensor_copy(ysm[half, 0:PAIRS, bass.ds(it - S_FIRST, 1)], psum[half, 7, 64 + h:80:2].rearrange("p (j a) -> p j a", a=1)).then_inc(sem("sa_ended"), 1)

            nothing = lambda it: None
            split_weights(0, S_FIRST, nothing, nothing)
            dve.sem_inc(sem("sa_scored"), 1)
            split_weights(S_FIRST, S_FIRST + NB, sample_scores, sample_softmax)
            split_weights(S_FIRST + NB, NZ // 2, nothing, nothing)

            def visit(n_, s_):
                for n, s in both(n_, s_):
                    kind, j = pairs[n]
                    ch, turn = chunks_of(kind), turn_step(chunks_of(kind))
                    for half in range(2):
                        if turn[last_chunk(ch, 4 * half + 3)] + 1 == s:
                            pair_wait(dve, "summed", n, last_chunk(ch, 4 * half + 3) + 1)
                            if n or half:
                                dve.wait_ge(sem("y_split"), 2 * n + half)
                            if half == 0:
                                dve.wait_ge(sem("zg_loaded"), 16 * (n + 1))
                            dve.tensor_tensor(yt[:], psum[:, 6, :], zg[:, 512 * half:512 * half + 512], ALU.mult).then_inc(sem(kind + "y_gated"), 1)
                    for c, (b, k0, nk) in enumerate(ch):
                        if turn[c] == s:
                            pair_wait(dve, "turned", n, 2 * c + 2)
                            buffer_wait(dve, "summed", n, c)
                            dve.tensor_copy(prob_t[:, 1, 0:nk], psum[:, 5, 0:nk]).then_inc(sem(kind + "copied1"), 1)
                    for b in range(QB):
                        if last_chunk(ch, b) + lag(ch, b) - 1 == s:
                            pair_wait(dve, "exped", n, 2 * b + 2)
                            m = mx[:, b % 4]
                            den = m[:, 6:8]
                            if kind == "B":
                                chain(dve.tensor_tensor(m[:, 12:14], m[:, 6:8], m[:, 10:12], ALU.add))
                                den = m[:, 12:14]
                            chain(dve.reciprocal(m[:, 8:10], den))
                            w = (b + 1) * BLK - off(kind, b)
                            for h in range(2):
                                pr = prob_of(n, b)[:, h, 0:w]
                                dve.tensor_scalar(pr, pr, m[:, 8 + h:9 + h], None, ALU.mult).then_inc(sem(kind + "scaled"), 1)
                    if s == 0:
                        if kind == "B":
                            dve.wait_ge(sem("consts3"), 80)
                    if s == 0 or s == 3 and kind == "A":
                        if s and n == 0:
                            dve.wait_ge(sem("consts"), 64)
                        u = slice(0, S // 2) if s else slice(S // 2, S) if kind == "A" else slice(S - 2 * BLK, S)
                        for h in range(2):
                            chain(dve.scalar_tensor_tensor(bias[:, h, u], negd[:, u], slope[:, 2 * j + h:2 * j + h + 1], mask[:, u], ALU.mult, ALU.add))
                        dve.sem_inc(sem("bias_built"), 1)
                    if s < len(ch):
                        b, k0, nk = ch[s]
                        m = mx[:, b % 4]
                        part = s - (last_chunk(ch, b - 1) + 1 if b else 0)
                        u0 = k0 - b * BLK + S - BLK
                        for h in range(2):
                            pair_wait(dve, "scored", n, 2 * s + h + 1)
                            place_wait(dve, n, b)
                            dve.tensor_tensor_reduce(prob_of(n, b)[:, h, k0 - off(kind, b):k0 - off(kind, b) + nk], psum[:, 2 * h + s % 2, 0:nk],
                                                     bias[:, h, u0:u0 + nk], SCALE, -3e38, ALU.add, ALU.max, m[:, 2 * part + h:2 * part + h + 1]).then_inc(sem(kind + "biased"), 1)
                        if s == last_chunk(ch, b):
                            pair_wait(dve, "biased", n, 2 * s + 2)
                            if part:
                                chain(dve.tensor_tensor(m[:, 0:2], m[:, 0:2], m[:, 2:4], ALU.max))
                            if kind == "B":
                                chain(dve.tensor_tensor(m[:, 0:2], m[:, 0:2], sink[:, 2 * j:2 * j + 2], ALU.max))
                            dve.tensor_scalar(m[:, 4:6], m[:, 0:2], -1.0, None, ALU.mult).then_inc(sem(kind + "shifted"), 1)
            dve.wait_ge(sem("produced"), 3 * (2 + NZ))
            dve.wait_ge(sem("z_stored0"), 16 * (NZ // 2 + 1))
            dve.wait_ge(sem("z_stored1"), 16 * (NZ // 2 + 1))
            for par in range(2):
                for h in range(2):
                    other = slice(HD * (1 - h), HD * (1 - h) + HD)
                    dve.memset(zq[other, par, h, :], 0.0).then_inc(sem("q_zeroed"), 1)
            dve.wait_ge(sem("consts3"), 64)
            walk(visit)

            heads = lambda ap: ap.rearrange("p (h d) -> p h d", d=HD)

            def kv_times_q(n, dst, k_row, q_row):
                for g in range(KVH):
                    four = slice(256 * g, 256 * g + 256)
                    m = dve.tensor_tensor(heads(dst[:, four]), heads(k_row[:, HD * g:HD * (g + 1)]).to_broadcast([n, 4, HD]), heads(q_row[:, four]), ALU.mult)
                return m
            dve.wait_ge(sem("b_copied"), 3)
            zr = zn[:].rearrange("p c n -> p (c n)")
            chain(kv_times_q(NB, bprod[0:NB], zr[:, S:S + 256], zr[:, 0:S]))
            dve.tensor_reduce(bnew[:], heads(bprod[0:NB]), AX.X, ALU.add).then_inc(sem("bnew_scored"), 1)
            dve.wait_ge(sem("bnew_scored"), 1)
            dve.wait_ge(sem("kb_loaded"), 16)
            for b in range(NB):
                dve.wait_ge(sem(f"qb_loaded{b}"), 16)
                chain(kv_times_q(P, bprod[:], kb[:, b, :], q_ring[:, b % 4, :]))
                dve.tensor_reduce(bsc[:, b, :], heads(bprod[:]), AX.X, ALU.add).then_inc(sem("b_scored"), 1)
                dve.wait_ge(sem("b_scored"), b + 1)
            dve.wait_ge(sem("b_rowed"), NB)
            dve.wait_ge(sem("bnew_rowed"), 1)
            seqs = lambda row: row.rearrange("p (b a) -> p b a", a=1).to_broadcast([HEADS, NB, NKB])
            for half in range(2):
                for_b = slice(4 * half, 4 * half + 4)
                dve.tensor_tensor(bprob[:, for_b, 0:P], psum[0:HEADS, half, :].rearrange("p (b k) -> p b k", b=4),
                                  bbias[:, 0:P].rearrange("p (a k) -> p a k", a=1).to_broadcast([HEADS, 4, P]), ALU.add)
            chain(dve.tensor_scalar(bprob[:, :, P:NKB], psum[0:HEADS, 3, 0:NB].rearrange("p (b a) -> p b a", a=1), bbias[:, P:NKB], None, ALU.add))
            chain(dve.tensor_scalar(bprob[:], bprob[:], SCALE, None, ALU.mult))
            chain(dve.tensor_reduce(brow[:, 0, :], bprob[:], AX.X, ALU.max))
            chain(dve.tensor_scalar(brow[:, 1, :], brow[:, 0, :], ssink[:], None, ALU.max))
            chain(dve.tensor_scalar(brow[:, 3, :], brow[:, 1, :], -1.0, None, ALU.mult))
            dve.tensor_scalar(brow[:, 2, :], brow[:, 3, :], ssink[:], None, ALU.add).then_inc(sem("b_shifted"), 1)
            dve.tensor_tensor(bprob[:], bprob[:], seqs(brow[:, 1, :]), ALU.subtract).then_inc(sem("b_shifted"), 2)
            dve.wait_ge(sem("b_exped"), 2)
            chain(dve.tensor_reduce(brow[:, 4, :], bprob[:], AX.X, ALU.add))
            chain(dve.tensor_tensor(brow[:, 4, :], brow[:, 4, :], brow[:, 2, :], ALU.add))
            chain(dve.reciprocal(brow[:, 5, :], brow[:, 4, :]))
            dve.tensor_tensor(bprob[:], bprob[:], seqs(brow[:, 5, :]), ALU.mult).then_inc(sem("b_scaled"), 1)
            dve.wait_ge(sem("b_pturned"), 1)
            dve.tensor_copy(bprob_t[:].rearrange("p b h -> p (b h)"), psum[:, 4, 0:P]).then_inc(sem("b_pcopied"), 1)
            dve.tensor_copy(bnew_t[:].rearrange("p b h -> p (b h)"), psum[0:1, 5, 0:P]).then_inc(sem("b_pcopied"), 1)
            dve.wait_ge(sem("b_summed"), 1)
            outs = psum[0:HD, 6, 0:P].rearrange("p (b j e) -> p e j b", b=NB, e=2)
            dve.wait_ge(sem("sa_ended"), 2 * NB)
            dve.tensor_copy(ysm[0:HD, PAIRS:KT, :], outs[:, 0])
            chain(dve.tensor_copy(ysm[HD:P, PAIRS:KT, :], outs[:, 1]))
            dve.tensor_tensor(ystmp[:, 0:8, :], ysm[:, 0:8, :], zst[:, ZGA:ZGA + 8, :], ALU.mult)
            chain(dve.tensor_tensor(ystmp[:, 8:16, :], ysm[:, 8:16, :], zst[:, ZGB:ZGB + 8, :], ALU.mult))
            chain(dve.tensor_copy(act_hi[:, :, S:R], ystmp[:]))
            dve.tensor_tensor(act_lo[:, :, S:R], ystmp[:], hi32[:, :, S:R], ALU.subtract).then_inc(sem("s_split"), 2)

            split_weights(NZ // 2, NT // 2, nothing, nothing)

            dve.wait_ge(sem("h_meaned"), 1)
            for t in range(3):
                dve.tensor_scalar(acc[:, T3 * t:T3 * (t + 1)], psum[:, t, 0:T3], 1.0 / D, EPS, ALU.mult, ALU.add).then_inc(sem("h_eps"), 1)
            for t in range(3):
                dve.wait_ge(sem("h_sqrt"), t + 1)
                dve.reciprocal(acc[:, T3 * t:T3 * (t + 1)], acc[:, T3 * t:T3 * (t + 1)]).then_inc(sem("h_rooted"), 1)
            def split_u(n):
                dve.wait_ge(sem("u_loaded"), 32 * (n + 1))
                if n >= 2:
                    dve.wait_ge(sem("u_produced"), 3 * (n - 1))
                dve.tensor_copy(u_hi[n % 2], u_raw[:]).then_inc(sem("u_hi_ready"), 1)
                dve.wait_ge(sem("u_hi_ready"), n + 1)
                dve.tensor_tensor(u_lo[n % 2], u_raw[:], u_hi[n % 2].bitcast(F32), ALU.subtract).then_inc(sem("u_lo_ready"), 1)
            for k in range(KT):
                dve.wait_ge(sem("h_hi"), k + 1)
                dve.scalar_tensor_tensor(act_lo[:, k, :], h_stage[:, k % 4, :], gcol[:, k:k + 1], hi32[:, k, :], ALU.mult, ALU.subtract).then_inc(sem("h_split"), 1)
                if k < len(ROW_TILES):
                    r0, n = ROW_TILES[k]
                    dve.wait_ge(sem("p_hi"), k + 1)
                    dve.tensor_tensor(pt_lo[:, :, r0:r0 + n], psum[:, 6 + k % 2, 0:2 * n].rearrange("p (m r) -> p m r", m=2),
                                      pt_hi[:, :, r0:r0 + n].bitcast(F32), ALU.subtract).then_inc(sem("p_lo"), 1)
                if k == 9:
                    split_u(0)
            dve.wait_ge(sem("h_split"), KT)
            dve.wait_ge(sem("h_rooted"), 3)
            for n in range(KT):
                if n + 1 < KT:
                    split_u(n + 1)
                for t in range(3):
                    u = 3 * n + t
                    rows = slice(T3 * t, T3 * (t + 1))
                    dve.wait_ge(sem("u_produced"), u + 1)
                    dve.tensor_tensor(t_gate[:, u % 2, :], psum[:, t, 0:T3], acc[:, rows], ALU.mult).then_inc(sem("g_scaled"), 1)
                    dve.wait_ge(sem("gated"), u + 1)
                    if u >= 2:
                        dve.wait_ge(sem("y_turned"), u - 1)
                    dve.tensor_tensor(t_y[:, u % 2, :], psum[:, 3 + t, 0:T3], t_gate[:, u % 2, :], ALU.mult).then_inc(sem("p_read"), 1)
                    dve.wait_ge(sem("p_read"), u + 1)
                    dve.wait_ge(sem(f"hin_loaded{u % 2}"), 16 * (u // 2 + 1))
                    dve.tensor_tensor(t_y[:, u % 2, :], t_y[:, u % 2, :], h_in[:, u % 2, :], ALU.add).then_inc(sem("h_added"), 1)
            dve.wait_ge(sem("gf_loaded"), 16)
            for i, (r0, n) in enumerate(ROW_TILES):
                dve.wait_ge(sem("f_squared"), i + 1)
                dve.tensor_scalar(small[0:n, 32 + i:33 + i], small[0:n, 32 + i:33 + i], 1.0 / D, EPS, ALU.mult, ALU.add).then_inc(sem("f_meaned"), 1)
                dve.wait_ge(sem("f_rooted"), i + 1)
                inverse_root(n, small[0:n, 32 + i:33 + i], small[0:n, 41 + i:42 + i], small[0:n, 50 + i:51 + i])
                dve.scalar_tensor_tensor(f_out[0:n, i % 2, :], f_in[0:n, i % 3, :], small[0:n, 50 + i:51 + i], gf_row[0:n, :],
                                         ALU.mult, ALU.mult).then_inc(sem("f_scaled"), 1)


_INS = ["x_prompt", "x_sample", "cache_a_k", "cache_a_v", "cache_b_k", "cache_b_v", "p_prompt", "p_sample",
        "g_mix", "w_in", "sinks", "w_out", "g_ple", "w_pg", "w_ple", "g_final"]
_OUTS = [(1, S, D), (NB, 1, D), (1, 1, S, HEADS, HD), (1, 1, S, HEADS, HD), (1, 1, P, KVH, HD), (1, 1, P, KVH, HD),
         (1, NB, 1, HEADS, HD), (1, NB, 1, HEADS, HD), (1, NB, 1, KVH, HD), (1, NB, 1, KVH, HD)]


def kernel(**inputs):
    import concourse.bacc as _bacc
    from concourse.bass_utils import run_bass_kernel_spmd as _run

    nc = _bacc.Bacc("TRN2", target_bir_lowering=False, num_devices=1)
    arrays, aps = {}, {}
    given = {n: np.ascontiguousarray(inputs[n]) for n in _INS}
    given.update(shape_tables())
    for name, x in given.items():
        arrays[f"in_{name}"] = x
        aps[name] = nc.dram_tensor(f"in_{name}", x.shape, F32, kind="ExternalInput").ap()
    outs = [nc.dram_tensor(f"out_{i}", s, F32, kind="ExternalOutput").ap() for i, s in enumerate(_OUTS)]
    build(nc, aps, outs)
    r = _run(nc, [arrays], core_ids=[0])
    return tuple(r.results[0][f"out_{i}"] for i in range(len(_OUTS)))
```
